# Optimizing a Trainium2 kernel written in Bass

```python
import jax
import jax.numpy as jnp
from jax import lax
import numpy as np

D_MODEL = 1024
BATCH = 1
SEQ = 1024
DEPTH = 1

HEAD_DIM = 64
MIX_WIDTH = D_MODEL
RWKV_WIDTH = 3 * D_MODEL // 8
LRU_WIDTH = D_MODEL // 4
SBA_WIDTH = MIX_WIDTH - RWKV_WIDTH - LRU_WIDTH
RWKV_HEADS = RWKV_WIDTH // HEAD_DIM
LRU_BLOCKS = LRU_WIDTH // HEAD_DIM
SBA_HEADS = SBA_WIDTH // HEAD_DIM

DECAY_RANK = 64
ICLR_RANK = 64
GATE_RANK = 128
RWKV_GN_EPS = 64e-5

CONV_WIDTH = 4
LRU_C = 8.0

SBA_BLOCK = 128

RWKV_COLS = 3 * RWKV_WIDTH + DECAY_RANK + ICLR_RANK + GATE_RANK
LRU_COLS = 2 * LRU_WIDTH
SBA_COLS = 3 * SBA_WIDTH
IN_COLS = RWKV_COLS + LRU_COLS + SBA_COLS

N_EXPERTS = 16
N_GROUPS = 4
EXPERTS_PER_GROUP = N_EXPERTS // N_GROUPS
TOP_K = 2
D_EXPERT = 512
MOE_BLOCK = 256

ALPHA = (2.0 * DEPTH) ** 0.25
BETA = (8.0 * DEPTH) ** -0.25
LN_EPS = 1e-5
RMS_EPS = 1e-6

kernel_name = 'hymba_rwkv7_rglru_stickbreak_grouped_moe'

def layer_norm(x, g, b):
    xf = x.astype(jnp.float32)
    mu = jnp.mean(xf, -1, keepdims=True)
    var = jnp.mean(jnp.square(xf - mu), -1, keepdims=True)
    return ((xf - mu) * lax.rsqrt(var + LN_EPS) * g + b).astype(x.dtype)

def head_rms_norm(y, g, n_heads):
    bsz, seq, c = y.shape
    yh = y.reshape(bsz, seq, n_heads, c // n_heads)
    yh = yh * lax.rsqrt(jnp.mean(jnp.square(yh), -1, keepdims=True) + RMS_EPS)
    return yh.reshape(bsz, seq, c) * g

def token_shift(p, mu):
    prev = jnp.pad(p, ((0, 0), (1, 0), (0, 0)))[:, :-1]
    return p + mu * (prev - p)

def rwkv7_scan(r, w, k, v, kk, a):
    bsz, _, h, n = r.shape

    def step(state, inp):
        r_t, w_t, k_t, v_t, kk_t, a_t = inp
        sa = jnp.einsum('bhvk,bhk->bhv', state, -kk_t)
        state = (state * w_t[:, :, None, :]
                 + sa[..., None] * (kk_t * a_t)[:, :, None, :]
                 + v_t[..., None] * k_t[:, :, None, :])
        return state, jnp.einsum('bhvk,bhk->bhv', state, r_t)

    xs = tuple(jnp.moveaxis(t, 1, 0) for t in (r, w, k, v, kk, a))
    state0 = jnp.zeros((bsz, h, n, n), jnp.float32)
    _, o = lax.scan(step, state0, xs)
    return jnp.moveaxis(o, 0, 1)

def rwkv7_time_mix(p, w0, w_up, a0, a_up, g_up, k_k, k_a, r_k, ln_g, ln_b):
    bsz, seq, _ = p.shape
    c = RWKV_WIDTH
    r, k, v, dw, da, dg = jnp.split(
        p, [c, 2 * c, 3 * c, 3 * c + DECAY_RANK, 3 * c + DECAY_RANK + ICLR_RANK], axis=-1)
    w_log = -jax.nn.softplus(-(w0 + jnp.tanh(dw) @ w_up)) - 0.5
    decay = jnp.exp(-jnp.exp(w_log))
    a = jax.nn.sigmoid(a0 + da @ a_up)
    g = jax.nn.sigmoid(dg) @ g_up

    def heads(t):
        return t.reshape(bsz, seq, RWKV_HEADS, HEAD_DIM)

    kk = heads(k * k_k)
    kk = kk / jnp.maximum(jnp.sqrt(jnp.sum(kk * kk, -1, keepdims=True)), 1e-12)
    k = k * (1.0 + (a - 1.0) * k_a)
    rh, kh, vh = heads(r), heads(k), heads(v)
    o = rwkv7_scan(rh, heads(decay), kh, vh, kk, heads(a))
    mu = jnp.mean(o, -1, keepdims=True)
    var = jnp.mean(jnp.square(o - mu), -1, keepdims=True)
    o = ((o - mu) * lax.rsqrt(var + RWKV_GN_EPS)).reshape(bsz, seq, c) * ln_g + ln_b
    bonus = jnp.sum(rh * kh * r_k.reshape(RWKV_HEADS, HEAD_DIM), -1, keepdims=True) * vh
    return (o + bonus.reshape(bsz, seq, c)) * g

def rglru_mix(p, conv_w, conv_b, wa, ba, wx, bx, lam, norm_g):
    bsz, seq, _ = p.shape
    gate_in, xin = jnp.split(p, [LRU_WIDTH], axis=-1)
    xc = lax.conv_general_dilated(
        xin, conv_w.astype(jnp.float32)[:, None, :], window_strides=(1,),
        padding=((CONV_WIDTH - 1, 0),), dimension_numbers=('NWC', 'WIO', 'NWC'),
        feature_group_count=LRU_WIDTH) + conv_b
    xb = xc.reshape(bsz, seq, LRU_BLOCKS, HEAD_DIM)
    gate_a = jax.nn.sigmoid(jnp.einsum('bsgi,gij->bsgj', xb, wa).reshape(bsz, seq, LRU_WIDTH) + ba)
    gate_x = jax.nn.sigmoid(jnp.einsum('bsgi,gij->bsgj', xb, wx).reshape(bsz, seq, LRU_WIDTH) + bx)
    log_a = -LRU_C * gate_a * jax.nn.softplus(-lam)
    a = jnp.exp(log_a)
    b_in = jnp.sqrt(-jnp.expm1(2.0 * log_a)) * (gate_x * xc)

    def combine(left, right):
        a1, b1 = left
        a2, b2 = right
        return a1 * a2, a2 * b1 + b2

    _, h = lax.associative_scan(combine, (a, b_in), axis=1)
    y = jax.nn.gelu(gate_in) * h
    return head_rms_norm(y, norm_g, LRU_BLOCKS)

def stick_breaking_attention(p, norm_g):
    bsz, seq, _ = p.shape
    q, k, v = jnp.split(p, [SBA_WIDTH, 2 * SBA_WIDTH], axis=-1)

    def heads(t):
        return jnp.transpose(t.reshape(bsz, seq, SBA_HEADS, HEAD_DIM), (0, 2, 1, 3))

    q, k, v = heads(q), heads(k), heads(v)
    scale = HEAD_DIM ** -0.5
    outs = []
    for i in range(seq // SBA_BLOCK):
        q0 = i * SBA_BLOCK
        kv_len = q0 + SBA_BLOCK
        z = jnp.einsum('bhtd,bhsd->bhts', q[:, :, q0:kv_len], k[:, :, :kv_len]) * scale
        t_idx = q0 + jnp.arange(SBA_BLOCK)[:, None]
        s_idx = jnp.arange(kv_len)[None, :]
        mask = s_idx < t_idx
        log_keep = jnp.where(mask, jax.nn.log_sigmoid(-z), 0.0)
        after = lax.cumsum(log_keep, axis=3, reverse=True) - log_keep
        attn = jnp.where(mask, jnp.exp(jax.nn.log_sigmoid(z) + after), 0.0)
        outs.append(jnp.einsum('bhts,bhsd->bhtd', attn, v[:, :, :kv_len]))
    o = jnp.concatenate(outs, axis=2)
    o = jnp.transpose(o, (0, 2, 1, 3)).reshape(bsz, seq, SBA_WIDTH)
    return head_rms_norm(o, norm_g, SBA_HEADS)

def grouped_moe(x2d, router_w, router_b, w_gate, w_up, w_down):
    n_tok, d = x2d.shape
    scores = jax.nn.softmax(x2d.astype(jnp.float32) @ router_w.astype(jnp.float32) + router_b, axis=-1)
    grouped = scores.reshape(n_tok, N_GROUPS, EXPERTS_PER_GROUP)
    group_score = jnp.sum(lax.top_k(grouped, TOP_K)[0], -1)
    sel = jnp.argmax(group_score, -1).astype(jnp.int32)
    cand = jnp.take_along_axis(grouped, sel[:, None, None], axis=1)[:, 0]
    top_vals, top_idx = lax.top_k(cand, TOP_K)
    expert_ids = sel[:, None] * EXPERTS_PER_GROUP + top_idx.astype(jnp.int32)
    gates = top_vals / jnp.sum(top_vals, -1, keepdims=True)

    n_assign = n_tok * TOP_K
    flat_e = expert_ids.reshape(n_assign)
    flat_tok = jnp.repeat(jnp.arange(n_tok, dtype=jnp.int32), TOP_K)
    flat_g = gates.reshape(n_assign)
    order = jnp.argsort(flat_e)
    se = flat_e[order]
    counts = jnp.bincount(flat_e, length=N_EXPERTS)
    starts = jnp.cumsum(counts) - counts
    padded = (counts + MOE_BLOCK - 1) // MOE_BLOCK * MOE_BLOCK
    pad_ends = jnp.cumsum(padded)
    pad_starts = pad_ends - padded
    dest = pad_starts[se] + jnp.arange(n_assign, dtype=jnp.int32) - starts[se]
    cap = n_assign + N_EXPERTS * MOE_BLOCK
    n_blocks = cap // MOE_BLOCK
    buf_tok = jnp.zeros((cap,), jnp.int32).at[dest].set(flat_tok[order])
    buf_gate = jnp.zeros((cap,), jnp.float32).at[dest].set(flat_g[order])
    block_e = jnp.minimum(
        jnp.searchsorted(pad_ends, jnp.arange(n_blocks, dtype=jnp.int32) * MOE_BLOCK, side='right'),
        N_EXPERTS - 1)

    def expert_block(acc, blk):
        tok, e, g = blk
        xb = x2d[tok]
        h = jax.nn.silu(xb @ w_gate[e]) * (xb @ w_up[e])
        yb = (h @ w_down[e]) * g[:, None]
        return acc.at[tok].add(yb.astype(acc.dtype)), None

    acc, _ = lax.scan(expert_block, jnp.zeros_like(x2d),
                      (buf_tok.reshape(n_blocks, MOE_BLOCK), block_e,
                       buf_gate.reshape(n_blocks, MOE_BLOCK)))
    return acc

def setup_inputs(seed: int = 0) -> dict:
    key = jax.random.key(seed)
    ks = jax.random.split(key, 40)
    f32 = jnp.float32
    L = DEPTH

    def nrm(k, shape, scale):
        return jax.random.normal(k, shape, f32) * scale

    u = jax.random.uniform(ks[20], (L, LRU_WIDTH), f32, 0.9, 0.999)
    p_lam = u ** (1.0 / LRU_C)
    return {
        'x': nrm(ks[0], (BATCH, SEQ, D_MODEL), 1.0),
        'w_in': nrm(ks[1], (L, D_MODEL, IN_COLS), D_MODEL ** -0.5),
        'shift_mu': jax.random.uniform(ks[2], (L, RWKV_COLS), f32),
        'rwkv_w0': jax.random.uniform(ks[3], (L, RWKV_WIDTH), f32, -6.0, 1.0),
        'rwkv_w_up': nrm(ks[4], (L, DECAY_RANK, RWKV_WIDTH), 0.5 * DECAY_RANK ** -0.5),
        'rwkv_a0': nrm(ks[5], (L, RWKV_WIDTH), 0.5),
        'rwkv_a_up': nrm(ks[6], (L, ICLR_RANK, RWKV_WIDTH), 0.5 * ICLR_RANK ** -0.5),
        'rwkv_g_up': nrm(ks[7], (L, GATE_RANK, RWKV_WIDTH), GATE_RANK ** -0.5),
        'rwkv_k_k': 0.85 + nrm(ks[8], (L, RWKV_WIDTH), 0.02),
        'rwkv_k_a': 1.0 + nrm(ks[9], (L, RWKV_WIDTH), 0.02),
        'rwkv_r_k': nrm(ks[10], (L, RWKV_WIDTH), 0.1),
        'rwkv_ln_g': 1.0 + nrm(ks[11], (L, RWKV_WIDTH), 0.02),
        'rwkv_ln_b': nrm(ks[12], (L, RWKV_WIDTH), 0.02),
        'lru_conv_w': nrm(ks[13], (L, CONV_WIDTH, LRU_WIDTH), CONV_WIDTH ** -0.5),
        'lru_conv_b': nrm(ks[14], (L, LRU_WIDTH), 0.02),
        'lru_wa': nrm(ks[15], (L, LRU_BLOCKS, HEAD_DIM, HEAD_DIM), HEAD_DIM ** -0.5),
        'lru_ba': nrm(ks[16], (L, LRU_WIDTH), 0.02),
        'lru_wx': nrm(ks[17], (L, LRU_BLOCKS, HEAD_DIM, HEAD_DIM), HEAD_DIM ** -0.5),
        'lru_bx': nrm(ks[18], (L, LRU_WIDTH), 0.02),
        'lru_lambda': jnp.log(p_lam) - jnp.log1p(-p_lam),
        'lru_norm_g': 1.0 + nrm(ks[19], (L, LRU_WIDTH), 0.02),
        'sba_norm_g': 1.0 + nrm(ks[21], (L, SBA_WIDTH), 0.02),
        'w_out': nrm(ks[22], (L, MIX_WIDTH, D_MODEL), MIX_WIDTH ** -0.5 * BETA),
        'ln1_g': 1.0 + nrm(ks[23], (L, D_MODEL), 0.02),
        'ln1_b': nrm(ks[24], (L, D_MODEL), 0.02),
        'ln2_g': 1.0 + nrm(ks[25], (L, D_MODEL), 0.02),
        'ln2_b': nrm(ks[26], (L, D_MODEL), 0.02),
        'router_w': nrm(ks[27], (D_MODEL, N_EXPERTS), D_MODEL ** -0.5),
        'router_b': nrm(ks[28], (N_EXPERTS,), 0.01),
        'exp_w_gate': nrm(ks[29], (L, N_EXPERTS, D_MODEL, D_EXPERT), D_MODEL ** -0.5),
        'exp_w_up': nrm(ks[30], (L, N_EXPERTS, D_MODEL, D_EXPERT), D_MODEL ** -0.5),
        'exp_w_down': nrm(ks[31], (L, N_EXPERTS, D_EXPERT, D_MODEL), D_EXPERT ** -0.5 * BETA),
    }

def reference(x, w_in, shift_mu, rwkv_w0, rwkv_w_up, rwkv_a0, rwkv_a_up, rwkv_g_up,
              rwkv_k_k, rwkv_k_a, rwkv_r_k, rwkv_ln_g, rwkv_ln_b, lru_conv_w, lru_conv_b,
              lru_wa, lru_ba, lru_wx, lru_bx, lru_lambda, lru_norm_g, sba_norm_g, w_out,
              ln1_g, ln1_b, ln2_g, ln2_b, router_w, router_b, exp_w_gate, exp_w_up,
              exp_w_down):
    bsz, seq, d = x.shape
    f32 = jnp.float32
    for l in range(DEPTH):
        p = x @ w_in[l]
        p_rwkv = token_shift(p[..., :RWKV_COLS].astype(f32), shift_mu[l])
        y_rwkv = rwkv7_time_mix(p_rwkv, rwkv_w0[l], rwkv_w_up[l], rwkv_a0[l], rwkv_a_up[l],
                                rwkv_g_up[l], rwkv_k_k[l], rwkv_k_a[l], rwkv_r_k[l],
                                rwkv_ln_g[l], rwkv_ln_b[l])
        y_lru = rglru_mix(p[..., RWKV_COLS:RWKV_COLS + LRU_COLS].astype(f32), lru_conv_w[l],
                          lru_conv_b[l], lru_wa[l], lru_ba[l], lru_wx[l], lru_bx[l],
                          lru_lambda[l], lru_norm_g[l])
        y_sba = stick_breaking_attention(p[..., RWKV_COLS + LRU_COLS:].astype(f32), sba_norm_g[l])
        mix = jnp.concatenate([y_rwkv, y_lru, y_sba], axis=-1).astype(x.dtype) @ w_out[l]
        x = layer_norm(ALPHA * x + mix, ln1_g[l], ln1_b[l])
        moe = grouped_moe(x.reshape(bsz * seq, d), router_w, router_b, exp_w_gate[l],
                          exp_w_up[l], exp_w_down[l]).reshape(bsz, seq, d)
        x = layer_norm(ALPHA * x + moe, ln2_g[l], ln2_b[l])
    return x


_drawn_inputs = setup_inputs


def setup_inputs(seed=0):
    import zlib

    import numpy as np

    out = dict(_drawn_inputs(seed))
    spreads = {}
    factors = {'rwkv_w_up': 4.084,
     'rwkv_k_k': 6.346,
     'rwkv_k_a': 8.0,
     'rwkv_ln_g': 6.053,
     'rwkv_ln_b': 4.958,
     'lru_ba': 8.0,
     'lru_bx': 8.0,
     'lru_norm_g': 4.004,
     'sba_norm_g': 2.956,
     'ln2_g': 2.806,
     'ln2_b': 2.803,
     'router_b': 3.263}
    for name, (base, spread) in spreads.items():
        noise = np.random.default_rng([zlib.crc32(name.encode()), seed]).standard_normal(out[name].shape)
        drawn = base * np.exp(spread * noise) if base else spread * noise
        out[name] = jnp.asarray(drawn.astype(out[name].dtype))
    for name, factor in factors.items():
        out[name] = (out[name] * factor).astype(out[name].dtype)
    return out
```

```python
import math
from contextlib import ExitStack

import concourse.bass as bass
from concourse import mybir

F32 = mybir.dt.float32
BF16 = mybir.dt.bfloat16
I32 = mybir.dt.int32
U32 = mybir.dt.uint32
U8 = mybir.dt.uint8
ALU = mybir.AluOpType
ACT = mybir.ActivationFunctionType
AX = mybir.AxisListType

D = 1024
S = 1024
P = 128
NT = S // P
KT = D // P
RW_W, LRU_W, SBA_W = 384, 256, 384
HD = 64
C = 64
NPAIR = RW_W // P
RW_T, LRU_T, SBA_T = 11, 4, 6
CT = RW_T + LRU_T + SBA_T
V_COL = CT * P
IN_COLS = V_COL + SBA_W
HB = 512
E_N, E_G, G_E, E_F = 16, 4, 4, 512
FT = E_F // P
ALPHA = 2.0 ** 0.25
DECAY = math.exp(-0.5)
NQ = NT // 2
NB = NPAIR * NQ
LEVELS = 6
NEG = -1e30
ROWS = 2 * S + P
MAXB = 2 * S // P + E_N


def wait(e, sem, v):
    if v > 0:
        e.wait_ge(sem, v)


def layer_kernel(nc, t, out, stop=None):
    ctx = ExitStack()
    with ctx:
        def sb(name, shape, dt=F32):
            return ctx.enter_context(nc.sbuf_tensor(name, shape, dt))

        def sem(name):
            return ctx.enter_context(nc.semaphore(name))

        ident = sb("ident", [P, P])
        identb = sb("identb", [P, P], BF16)
        causal_neg = sb("causal_neg", [P, P], BF16)
        head_ones = sb("head_ones", [P, P])
        mask4 = sb("mask4", [P, 4, P], BF16)
        ident2 = sb("ident2", [P, C])
        lower = sb("lower", [P, LEVELS, P], U8)
        upper = sb("upper", [P, LEVELS, P], U8)
        restart = sb("restart", [P, S], BF16)
        vec = sb("vec", [P, 96])
        consts = sb("consts", [P, 8])
        w_up = sb("w_up", [P, RW_W])
        g_up = sb("g_up", [P, RW_W])
        lru_w = sb("lru_w", [P, 2, 2, HD])
        pc = sb("pc", [P, NPAIR, S // C])

        RW = sb("RW", [P, RW_T, S])
        KB = sb("KB", [P, 6, S])
        YT = sb("YT", [P, KT, S])
        SQ = sb("SQ", [P, 9, S])
        XS = sb("XS", [P, 12, S])
        TT = sb("TT", [P, 3, S])
        SV = SQ[:, 6:9, :].rearrange("p a b -> p (a b)").rearrange("p (n c) -> p n c", c=SBA_W)

        nvec = [0]

        def vcol(n):
            a = nvec[0]
            nvec[0] += n
            return a
        V_MU = vcol(RW_T)
        V_W0, V_A0, V_KK, V_KA, V_RK, V_LNG, V_LNB, V_SG = [vcol(3) for _ in range(8)]
        V_CW, V_CB, V_BA, V_BX, V_LAM, V_LG = vcol(8), vcol(2), vcol(2), vcol(2), vcol(2), vcol(2)
        V_LAST = nvec[0]
        V_NMU, V_NKA = vcol(RW_T), vcol(3)
        V_C, V_NC, V_L1, V_L2 = vcol(2), vcol(2), vcol(2), vcol(2)
        assert nvec[0] <= 96

        def v1(i):
            return vec[:, i:i + 1]

        PS = [ctx.enter_context(nc.psum_tensor(f"PS{i}", [P, 2 * HB], F32)) for i in range(4)]

        s_const = sem("consts_loaded")
        s_derived = sem("derived_consts_dve")
        s_lamc = sem("lambda_steps_act")
        s_masks = sem("masks_built_pool")
        s_masksd = sem("masks_built_dve")
        s_x = [sem(f"x_loaded{i}") for i in range(NT)]
        s_w = [sem(f"w_in_loaded{i}") for i in range(4)]
        s_pp = sem("proj_in_psum")
        s_pa = sem("shift_kept_by_act")
        s_pd = sem("shift_done_by_dve")
        s_pe = sem("proj_copied_by_act")
        s_ld, s_la, s_lp = sem("lru_dve"), sem("lru_act"), sem("lru_pe")
        s_rd, s_ra, s_rp = sem("rwkv_dve"), sem("rwkv_act"), sem("rwkv_pe")
        s_md, s_ma, s_mp, s_mo = sem("delta_dve"), sem("delta_act"), sem("delta_pe"), sem("delta_pool")
        s_wo, s_rc, s_op = sem("w_out_loaded"), sem("router_consts_loaded"), sem("mixed_in_psum")
        s_xr = [sem(f"x_rows_loaded{i}") for i in range(4)]
        s_n1d, s_n1a = sem("norm1_dve"), sem("norm1_act")
        s_x1p, s_x1t, s_lg = sem("x1_transposed"), sem("x1T_copied"), sem("logits_in_psum")
        s_rpool, s_q, s_qd, s_qa, s_qp = [sem(f"router_{x}") for x in ("pool", "chain", "dve", "act", "pe")]
        s_slot, s_tab, s_sc = sem("slots_ready"), sem("block_table_ready"), sem("rows_dispatched")
        s_wg, s_wu, s_wd = [[sem(f"{x}_loaded{k}") for k in range(2)] for x in ("w_gate", "w_up", "w_down")]
        s_xg, s_xgp, s_ta, s_td = sem("block_rows"), sem("block_transposed"), sem("xgT_act"), sem("xgT_dve")
        s_g1, s_u1, s_si, s_hd = sem("gate_in_psum"), sem("up_in_psum"), sem("silu_done"), sem("hidden_done")
        s_htp, s_htd, s_y1 = sem("hidden_transposed"), sem("hiddenT_copied"), sem("down_in_psum")
        s_ya, s_yd, s_ys = sem("y_act"), sem("y_dve"), sem("y_stored")
        s_gt = [sem(f"y_gathered{i}") for i in range(12)]
        s_tick = [sem("sp_passed_wait"), sem("pool_passed_wait")]
        s_l2, s_n2d, s_n2a, s_out = sem("norm2_consts"), sem("norm2_dve"), sem("norm2_act"), sem("out_stored")
        s_init = sem("identities_set")
        s_tl, s_ul = sem("inverse_level"), sem("inverse_transposed_level")
        s_bz, s_bx, s_bv = sem("z_in_psum"), sem("attn_transposed"), sem("attn_v_in_psum")
        s_bd, s_ba, s_bt, s_bo = sem("attn_dve"), sem("attn_act"), sem("attnT_copied"), sem("attn_out_copied")
        s_na, s_np, s_nd = sem("head_norm_act"), sem("head_norm_pe"), sem("head_norm_dve")
        s_fd, s_fa, s_fp = sem("rwkv_norm_dve"), sem("rwkv_norm_act"), sem("rwkv_norm_pe")

        const_loads = [(vec[:, 0:V_LAST], t["vecs"]), (w_up[:, :], t["lora_up"]), (g_up[:, :], t["g_up"]),
                       (lru_w[:, :, :, :], t["lru_w"])]
        CONSTS = 16 * len(const_loads)

        block = ctx.enter_context(nc.Block())

        def proj_sp(e):
            for ct in range(CT):
                if ct >= 4:
                    wait(e, s_pp, ct - 3)
                e.dma_start(XS[:, 8 + ct % 4, :], t["w_in"][ct]).then_inc(s_w[ct % 4], 16)
                if ct == 0:
                    for kt in range(KT):
                        e.dma_start(XS[:, kt, :], t["xT"][kt]).then_inc(s_x[kt], 16)
            wait(e, s_pp, CT - 1)
            e.dma_start(XS[:, 9:12, :].rearrange("p a b -> p (a b)"), t["w_v"]).then_inc(s_w[1], 16)

        def proj_free(e, n):
            if n >= 2:
                if n - 2 < RW_T:
                    wait(e, s_pd, n - 1)
                else:
                    wait(e, s_pe, n - 1 - RW_T)

        def proj_pe(e, n):
            proj_free(e, n)
            acc = PS[n % 2]
            if n < CT:
                wait(e, s_w[n % 4], 16 * (n // 4 + 1))
                for half in range(2):
                    for kt in range(KT):
                        if n == 0 and half == 0:
                            wait(e, s_x[kt], 16)
                        m = e.matmul(acc[:, half * HB:(half + 1) * HB], XS[:, 8 + n % 4, kt * P:(kt + 1) * P],
                                     XS[:, kt, half * HB:(half + 1) * HB], start=kt == 0, stop=kt == KT - 1)
            else:
                i = n - CT
                if i == 0:
                    wait(e, s_w[1], 16 * 6)
                wv = XS[:, 9:12, :].rearrange("p a b -> p (a b)").rearrange("p (k c) -> p k c", k=KT)
                for kt in range(KT):
                    m = e.matmul(acc[:, 0:SBA_W], XS[:, kt, i * P:(i + 1) * P], wv[:, kt, :],
                                 start=kt == 0, stop=kt == KT - 1)
            m.then_inc(s_pp, 1)

        def proj_act(e, n):
            if n == 0:
                wait(e, s_derived, 1)
            wait(e, s_pp, n + 1)
            if n < RW_T:
                e.activation(RW[:, n, :], PS[n % 2][:, :], ACT.Identity,
                             scale=v1(V_NMU + n)).then_inc(s_pa, 1)
            elif n < RW_T + LRU_T:
                e.copy(YT[:, 3 + n - RW_T, :], PS[n % 2][:, :]).then_inc(s_pe, 1)
            elif n < RW_T + LRU_T + NPAIR:
                e.mul(SQ[:, n - RW_T - LRU_T, :], PS[n % 2][:, :], HD ** -0.5).then_inc(s_pe, 1)
            elif n < CT:
                e.copy(SQ[:, n - RW_T - LRU_T, :], PS[n % 2][:, :]).then_inc(s_pe, 1)
            else:
                e.copy(SV[:, n - CT, :], PS[n % 2][:, 0:SBA_W]).then_inc(s_pe, 1)

        def proj_dve(e, n):
            wait(e, s_pa, n + 1)
            e.scalar_tensor_tensor(RW[:, n, 1:S], PS[n % 2][:, 0:S - 1], v1(V_MU + n), RW[:, n, 1:S],
                                   ALU.mult, ALU.add).then_inc(s_pd, 1)

        LD, LA, LP = 14, 12, 3

        def exp_ln(e):
            e.preload_act_table_set("natural_log_exp_and_others")

        def lru_bufs(u):
            return KB[:, 3 * u, :], KB[:, 3 * u + 1, :], KB[:, 3 * u + 2, :], TT[:, u, :], YT[:, 3 + u, :], YT[:, 5 + u, :]

        def lru_dve(e, u):
            A, B, Cc, Dd, G, X = lru_bufs(u)
            n = [u * LD]

            def step(ins):
                ins.then_inc(s_ld, 1)
                n[0] += 1
                return n[0]

            def own():
                wait(e, s_ld, n[0])
            wait(e, s_pe, LRU_T)
            own()
            step(e.tensor_scalar(A, X, v1(V_CW + 2 * 3 + u), v1(V_CB + u), ALU.mult, ALU.add))
            for back in range(1, 4):
                own()
                step(e.scalar_tensor_tensor(A[:, back:S], X[:, 0:S - back], v1(V_CW + 2 * (3 - back) + u),
                                            A[:, back:S], ALU.mult, ALU.add))
            wait(e, s_la, u * LA + 1)
            own()
            step(e.tensor_scalar(B, B, 0.044715, 1.0, ALU.mult, ALU.add))
            own()
            step(e.tensor_tensor(B, B, G, ALU.mult))
            wait(e, s_la, u * LA + 2)
            own()
            step(e.scalar_tensor_tensor(G, B, 1.0, G, ALU.add, ALU.mult))
            wait(e, s_la, u * LA + 4)
            own()
            step(e.tensor_tensor(Dd, Dd, A, ALU.mult))
            wait(e, s_la, u * LA + 5)
            own()
            step(e.tensor_scalar_max(B, B, 2.0 ** -62))
            wait(e, s_la, u * LA + 8)
            own()
            step(e.tensor_tensor(A, X, A, ALU.subtract))
            wait(e, s_la, u * LA + 9)
            own()
            step(e.tensor_tensor(Dd, Dd, A, ALU.mult))
            own()
            step(e.tensor_tensor_scan(A, Cc, Dd, 0.0, ALU.mult, ALU.add))
            own()
            step(e.scalar_tensor_tensor(A, G, 0.5, A, ALU.mult, ALU.mult))
            wait(e, s_la, u * LA + 12)
            own()
            step(e.scalar_tensor_tensor(G, A, v1(V_LG + u), B, ALU.mult, ALU.mult))

        def lru_act(e, u, part):
            A, B, Cc, Dd, G, X = lru_bufs(u)
            if part == 0:
                wait(e, s_pe, LRU_T)
                wait(e, s_la, u * LA + 0)
                e.activation(B, G, ACT.Square).then_inc(s_la, 1)
                wait(e, s_ld, u * LD + 6)
                wait(e, s_la, u * LA + 1)
                e.activation(B, B, ACT.Tanh, scale=0.7978845608028654).then_inc(s_la, 1)
                wait(e, s_lp, u * LP + 1)
                wait(e, s_la, u * LA + 2)
                e.activation(Cc, PS[2][:, :], ACT.Sigmoid, bias=v1(V_BA + u)).then_inc(s_la, 1)
                wait(e, s_lp, u * LP + 2)
                wait(e, s_la, u * LA + 3)
                e.activation(Dd, PS[3][:, :], ACT.Sigmoid, bias=v1(V_BX + u)).then_inc(s_la, 1)
                wait(e, s_ld, u * LD + 7)
                wait(e, s_masksd, 1)
                wait(e, s_la, u * LA + 4)
                e.activation(B, Cc, ACT.Tanh, scale=v1(V_C + u)).then_inc(s_la, 1)
                return
            exp_ln(e)
            wait(e, s_la, u * LA + 5)
            e.activation(Cc, Cc, ACT.Exp, scale=v1(V_NC + u)).then_inc(s_la, 1)
            wait(e, s_ld, u * LD + 9)
            wait(e, s_la, u * LA + 6)
            e.activation(A, B, ACT.Ln, bias=1.0).then_inc(s_la, 1)
            wait(e, s_la, u * LA + 7)
            e.activation(X, B, ACT.Ln, scale=2.0).then_inc(s_la, 1)
            wait(e, s_ld, u * LD + 10)
            wait(e, s_la, u * LA + 8)
            e.activation(A, A, ACT.Exp, scale=0.5).then_inc(s_la, 1)
            wait(e, s_ld, u * LD + 13)
            wait(e, s_la, u * LA + 9)
            e.activation(B, A, ACT.Square).then_inc(s_la, 1)
            wait(e, s_lp, u * LP + 3)
            wait(e, s_la, u * LA + 10)
            e.activation(B, PS[2][:, :], ACT.Ln, scale=1.0 / HD, bias=consts[:, 0:1]).then_inc(s_la, 1)
            wait(e, s_la, u * LA + 11)
            e.activation(B, B, ACT.Exp, scale=-0.5).then_inc(s_la, 1)

        def heads_sum(e, acc, src):
            for half in range(2):
                m = e.matmul(acc[:, half * HB:(half + 1) * HB], head_ones[:, :], src[:, half * HB:(half + 1) * HB],
                             start=True, stop=True)
            return m

        def lru_pe(e, u, part):
            A, B = lru_bufs(u)[0:2]
            if part < 2:
                if part == 0:
                    wait(e, s_masksd, 1)
                    wait(e, s_const, CONSTS)
                    wait(e, s_ld, u * LD + 4)
                    wait(e, s_la, (u - 1) * LA + 11 if u else 0)
                for half in range(2):
                    for b in range(2):
                        q = slice(b * HD, (b + 1) * HD)
                        m = e.matmul(PS[2 + part][q, half * HB:(half + 1) * HB], lru_w[q, part, u, :],
                                     A[q, half * HB:(half + 1) * HB], start=True, stop=True)
                m.then_inc(s_lp, 1)
                return
            wait(e, s_la, u * LA + 10)
            heads_sum(e, PS[2], B).then_inc(s_lp, 1)

        RD, RA, RP = 14, 8, 4

        def rw_bufs(g):
            T = [TT[:, i, :] for i in range(3)] if g != 1 else [YT[:, 5 + i, :] for i in range(3)]
            return T + [KB[:, g, :], KB[:, 3 + g, :], YT[:, g, :], RW[:, g, :], RW[:, 3 + g, :], RW[:, 6 + g, :]]

        def rw_pre_act(e):
            wait(e, s_pd, RW_T)
            e.activation(RW[0:HD, 9, :], RW[0:HD, 9, :], ACT.Tanh)
            e.activation(RW[:, 10, :], RW[:, 10, :], ACT.Sigmoid).then_inc(s_ra, 1)

        def rw_act(e, g, part):
            T1, T2, T3, K, B, Y, r, k, v = rw_bufs(g)
            a0, d0, p0 = g * RA + 1, g * RD, g * RP
            if part == 0:
                if g == 0:
                    wait(e, s_ld, 2 * LD)
                if g == 2:
                    wait(e, s_rd, RD)
                wait(e, s_rp, p0 + 1)
                wait(e, s_ra, a0 + 0)
                e.activation(T1, PS[2][:, :], ACT.Sigmoid, bias=v1(V_W0 + g)).then_inc(s_ra, 1)
                wait(e, s_rp, p0 + 2)
                wait(e, s_ra, a0 + 1)
                e.activation(T3, PS[3][:, :], ACT.Sigmoid, bias=v1(V_A0 + g)).then_inc(s_ra, 1)
                wait(e, s_ra, a0 + 2)
                e.activation(Y, k, ACT.Square, scale=v1(V_KK + g)).then_inc(s_ra, 1)
                return
            exp_ln(e)
            wait(e, s_rd, d0 + 1)
            wait(e, s_ra, a0 + 3)
            e.activation(Y, Y, ACT.Ln, scale=2.0 ** 16).then_inc(s_ra, 1)
            wait(e, s_ra, a0 + 4)
            e.activation(Y, Y, ACT.Exp, scale=-0.5, bias=consts[:, 1:2]).then_inc(s_ra, 1)
            wait(e, s_rd, d0 + 3)
            wait(e, s_ra, a0 + 5)
            e.activation(T1, T1, ACT.Exp, scale=-DECAY).then_inc(s_ra, 1)
            wait(e, s_rd, d0 + 7)
            wait(e, s_ra, a0 + 6)
            e.activation(T3, T2, ACT.Exp, scale=-DECAY).then_inc(s_ra, 1)
            wait(e, s_ra, a0 + 7)
            e.activation(T2, T2, ACT.Exp, scale=DECAY).then_inc(s_ra, 1)

        def rw_dve(e, g):
            T1, T2, T3, K, B, Y, r, k, v = rw_bufs(g)
            a0, d0, p0 = g * RA + 1, g * RD, g * RP
            n = [d0]

            def step(ins):
                ins.then_inc(s_rd, 1)
                n[0] += 1

            def own():
                wait(e, s_rd, n[0])
            wait(e, s_ra, a0 + 3)
            wait(e, s_rp, p0 + 3)
            own()
            step(e.tensor_scalar_max(Y, PS[2][:, :], 1e-24))
            own()
            step(e.tensor_tensor_scan(T2, restart[:, :], T1, 0.0, ALU.mult, ALU.add))
            own()
            step(e.tensor_tensor(T1, T2, T1, ALU.subtract))
            wait(e, s_ra, a0 + 5)
            own()
            step(e.scalar_tensor_tensor(K, k, v1(V_KK + g), Y, ALU.mult, ALU.mult))
            own()
            step(e.tensor_tensor(B, K, T3, ALU.mult))
            own()
            step(e.tensor_scalar(T3, T3, v1(V_KA + g), v1(V_NKA + g), ALU.mult, ALU.add))
            own()
            step(e.tensor_tensor(k, k, T3, ALU.mult))
            own()
            step(e.scalar_tensor_tensor(Y, r, v1(V_RK + g), k, ALU.mult, ALU.mult))
            wait(e, s_ra, a0 + 6)
            own()
            step(e.tensor_tensor(K, K, T1, ALU.mult))
            wait(e, s_rp, p0 + 4)
            own()
            step(e.tensor_tensor(Y, PS[3][:, :], v, ALU.mult))
            wait(e, s_ra, a0 + 7)
            own()
            step(e.tensor_tensor(r, r, T3, ALU.mult))
            own()
            step(e.tensor_copy(pc[:, g, :], T3[:, C - 1:S:C]))
            wait(e, s_ra, a0 + 8)
            own()
            step(e.tensor_tensor(B, B, T2, ALU.mult))
            own()
            step(e.tensor_tensor(k, k, T2, ALU.mult))

        def rw_pe(e, g, part):
            T1, T2, T3, K, B, Y, r, k, v = rw_bufs(g)
            a0, d0 = g * RA + 1, g * RD
            if part == 0:
                wait(e, s_ra, 1)
                if g == 0:
                    wait(e, s_la, 2 * LA)
                else:
                    wait(e, s_rd, d0 - RD + 10)
                for rows, acc in ((slice(0, HD), PS[2]), (slice(HD, P), PS[3])):
                    for half in range(2):
                        m = e.matmul(acc[:, half * HB:(half + 1) * HB], w_up[rows, g * P:(g + 1) * P],
                                     RW[rows, 9, half * HB:(half + 1) * HB], start=True, stop=True)
                    m.then_inc(s_rp, 1)
            elif part == 1:
                wait(e, s_ra, a0 + 3)
                heads_sum(e, PS[2], Y).then_inc(s_rp, 1)
            else:
                wait(e, s_rd, d0 + 8)
                heads_sum(e, PS[3], Y).then_inc(s_rp, 1)


        s_iota = sem("iotas_by_pool")
        ip = TT[:, 0, 0:P].bitcast(I32)
        jf = TT[:, 0, P:2 * P].bitcast(I32)
        xr = TT[:, 0, 2 * P:3 * P].bitcast(I32)
        xrf, dff, m1, m2 = [TT[:, 0, (3 + i) * P:(4 + i) * P] for i in range(4)]

        def masks_pool(e):
            e.memset(ident[:, :], 0.0)
            e.memset(causal_neg[:, :], 0.0)
            e.iota(ip, [[0, P]], base=0, channel_multiplier=1)
            e.iota(jf, [[1, P]], base=0, channel_multiplier=0).then_inc(s_iota, 1)
            e.wait_ge(s_iota, 1)
            e.affine_select(out=ident[:, :], in_=ident[:, :], compare_op=ALU.not_equal, fill=1.0, base=0,
                            pattern=[[-1, P]], channel_multiplier=1)
            e.affine_select(out=causal_neg[:, :], in_=causal_neg[:, :], compare_op=ALU.is_gt, fill=NEG, base=0,
                            pattern=[[-1, P]], channel_multiplier=1).then_inc(s_masks, 1)
            for dst, src in const_loads:
                e.dma_start(dst, src).then_inc(s_const, 16)

        def masks_dve(e):
            n = [0]
            s_own = sem("mask_steps_dve")

            def step(ins):
                ins.then_inc(s_own, 1)
                n[0] += 1
                e.wait_ge(s_own, n[0])
            step(e.memset(restart[:, :], 1.0))
            for i, x in enumerate((1e-6, 8 * math.log(2.0), 64e-5, 1e-5)):
                ins = e.memset(consts[:, i:i + 1], x)
            step(ins)
            step(e.memset(restart[:, 0:S:C], 0.0))
            wait(e, s_masks, 1)
            step(e.tensor_copy(identb[:, :], ident[:, :]))
            step(e.tensor_tensor(xr, ip, jf, ALU.bitwise_xor))
            step(e.tensor_copy(xrf, xr))
            step(e.tensor_tensor(dff, jf, ip, ALU.subtract))
            step(e.tensor_single_scalar(head_ones[:, :], xr, C, ALU.is_lt))
            step(e.tensor_tensor(ident2[:, :], ident[:, 0:C], ident[:, C:P], ALU.add))
            step(e.tensor_single_scalar(m1, dff, 0.0, ALU.is_gt))
            step(e.tensor_single_scalar(m2, dff, 0.0, ALU.is_ge))
            step(e.scalar_tensor_tensor(mask4[:, 0, :], m1, -1.0, head_ones[:, :], ALU.mult, ALU.mult))
            step(e.tensor_tensor(mask4[:, 1, :], m2, head_ones[:, :], ALU.mult))
            step(e.tensor_tensor(mask4[:, 2, :], m1, head_ones[:, :], ALU.mult))
            step(e.tensor_tensor(mask4[:, 3, :], m2, head_ones[:, :], ALU.mult))
            step(e.tensor_single_scalar(m2, dff, 0.0, ALU.is_lt))
            for lv in range(LEVELS):
                step(e.tensor_single_scalar(dff, xrf, float(1 << lv), ALU.is_ge))
                step(e.scalar_tensor_tensor(dff, xrf, float(2 << lv), dff, ALU.is_lt, ALU.mult))
                step(e.tensor_tensor(upper[:, lv, :], dff, m1, ALU.mult))
                step(e.tensor_tensor(lower[:, lv, :], dff, m2, ALU.mult))
            wait(e, s_const, CONSTS)
            e.tensor_scalar(vec[:, V_NMU:V_NMU + RW_T], vec[:, V_MU:V_MU + RW_T], -1.0, 1.0, ALU.mult, ALU.add)\
                .then_inc(s_derived, 1)
            step(e.tensor_scalar(vec[:, V_NKA:V_NKA + 3], vec[:, V_KA:V_KA + 3], -1.0, 1.0, ALU.mult, ALU.add))
            step(e.tensor_scalar(vec[:, V_C:V_C + 2], vec[:, V_LAM:V_LAM + 2], -1.0, 0.0, ALU.mult, ALU.max))
            e.wait_ge(s_lamc, 3)
            step(e.tensor_tensor(vec[:, V_C:V_C + 2], vec[:, V_C:V_C + 2], vec[:, V_L1:V_L1 + 2], ALU.add))
            step(e.tensor_scalar_mul(vec[:, V_NC:V_NC + 2], vec[:, V_C:V_C + 2], -8.0))
            step(e.tensor_scalar_mul(vec[:, V_C:V_C + 2], vec[:, V_C:V_C + 2], 8.0))
            e.tensor_copy(vec[:, V_L2:V_L2 + 2], vec[:, V_C:V_C + 2]).then_inc(s_masksd, 1)

        def lam_act(e):
            a = vec[:, V_L1:V_L1 + 2]
            wait(e, s_const, CONSTS)
            e.activation(a, vec[:, V_LAM:V_LAM + 2], ACT.Abs).then_inc(s_lamc, 1)
            e.wait_ge(s_lamc, 1)
            e.activation(a, a, ACT.Exp, scale=-1.0).then_inc(s_lamc, 1)
            e.wait_ge(s_lamc, 2)
            e.activation(a, a, ACT.Ln, bias=1.0).then_inc(s_lamc, 1)


        MP, MD, MA = 30, 10, 10
        NTL, NUL = LEVELS - 1, LEVELS

        def p_level(lv, what):
            return 8 + 3 * (lv - 1) + 1 + (what if lv < LEVELS - 1 else min(what, 1))
        P_T, P_HF, P_JG, P_ST = 23, 24, 25, 25
        XF = XS[:, :, :].rearrange("p a b -> p (a b)")
        off = [0]

        def lay(n):
            a = off[0]
            off[0] += n
            return XF[:, a:a + n]
        AM = lay(4 * 4 * P).rearrange("p (m k c) -> p m k c", m=4, k=4)
        T_ = lay(4 * P).rearrange("p (m c) -> p m c", m=4)
        U_ = lay(4 * P).rearrange("p (m c) -> p m c", m=4)
        M1 = lay(4 * P).rearrange("p (m c) -> p m c", m=4)
        RHS = lay(4 * P).rearrange("p (m c) -> p m c", m=4)
        WY = lay(4 * P).rearrange("p (m c) -> p m c", m=4)
        TOK = lay(2 * 3 * P).rearrange("p (i k c) -> p i k c", i=2, k=3)
        BKC = lay(2 * 2 * P).rearrange("p (k c) -> p k c", k=2)
        HF = lay(4 * P)
        JG = lay(4 * P)
        ST = lay(5 * C).rearrange("p (k c) -> p k c", k=5)
        Eb = [lay(S) for _ in range(2)]
        ATb = [lay(S) for _ in range(2)]
        assert off[0] <= 12 * S

        def RB(j):
            return PS[2 + j // 2][:, (j % 2) * HB:(j % 2 + 1) * HB]

        def four(x):
            return x.rearrange("p (m c) -> p m c", m=4)

        def mats_of(b):
            g, q = b // NQ, b % NQ
            return g, q, [(m, m // 2, slice((m % 2) * HD, (m % 2 + 1) * HD)) for m in range(4)]

        def mats_pool(e):
            for b in range(NB):
                g, q, _ = mats_of(b)
                wait(e, s_rd, RD * NPAIR)
                if b == 0:
                    wait(e, s_pp, CT + NT)
                wait(e, s_mp, (b - 1) * MP + 6 if b else 0)
                dec = pc[:, g, 4 * q:4 * q + 4].rearrange("p (n o) -> p n o", o=1).broadcast_to([P, 4, C])
                for k, src in enumerate((KB[:, 3 + g, :], RW[:, 3 + g, :])):
                    ins = e.tensor_tensor(BKC[:, k, :].rearrange("p (n c) -> p n c", c=C),
                                          src[:, 256 * q:256 * q + 256].rearrange("p (n c) -> p n c", c=C), dec,
                                          ALU.mult)
                ins.then_inc(s_mo, 1)
                wait(e, s_mp, (b - 1) * MP + P_T if b else 0)
                eye = ident[:, :].rearrange("p (o c) -> p o c", o=1).broadcast_to([P, 4, P])
                e.tensor_copy(T_[:, :, :], eye)
                e.tensor_copy(U_[:, :, :], eye).then_inc(s_init, 1)

        def mats_pe(e, b):
            g, q, ms = mats_of(b)
            P0, D0, A0 = b * MP, b * MD, b * MA
            Kq, Bt, Kt, Rt, V = KB[:, g, :], KB[:, 3 + g, :], RW[:, 3 + g, :], RW[:, g, :], RW[:, 6 + g, :]
            wait(e, s_rd, RD * NPAIR)
            wait(e, s_ra, RA * NPAIR + 1)
            wait(e, s_ma, A0)
            wait(e, s_fd, 4 * g)
            for m, i, h in ms:
                wait(e, s_md, D0 - (5, 1, 1, 0)[m] if b else 0)
                tk = slice((2 * q + i) * P, (2 * q + i + 1) * P)
                for k, (l, r) in enumerate(((Bt, Kq), (Bt, Rt), (Kt, Kq), (Kt, Rt))):
                    ins = e.matmul(RB(m)[:, k * P:(k + 1) * P], l[h, tk], r[h, tk], start=True, stop=True)
                ins.then_inc(s_mp, 1)
            wait(e, s_mo, b + 1)
            for i in range(2):
                wait(e, s_md, D0 + i + 1)
                tk = slice((2 * q + i) * P, (2 * q + i + 1) * P)
                for k, src in enumerate((Kq[:, tk], V[:, tk], BKC[:, 0, i * P:(i + 1) * P],
                                         BKC[:, 1, i * P:(i + 1) * P])):
                    ins = e.transpose(RB(i)[:, k * P:(k + 1) * P], src, ident[:, :])
                ins.then_inc(s_mp, 1)
            wait(e, s_md, D0 + 4)
            for m, i, h in ms:
                ins = e.transpose(RB(2)[:, m * P:(m + 1) * P], AM[:, m, 0, :], ident[:, :])
            ins.then_inc(s_mp, 1)
            yield
            wait(e, s_ma, A0 + 2)
            for m, i, h in ms:
                ins = e.matmul(RB(1)[:, m * HD:(m + 1) * HD], AM[:, m, 2, :], TOK[:, i, 0, h], start=True, stop=True)
            ins.then_inc(s_mp, 1)
            for lv in range(1, LEVELS):
                wait(e, s_tl, b * NTL + lv)
                for m, i, h in ms:
                    ins = e.matmul(RB(3)[:, m * P:(m + 1) * P], AM[:, m, 0, :], T_[:, m, :], start=True, stop=True)
                ins.then_inc(s_mp, 1)
                yield
                wait(e, s_ul, b * NUL + lv)
                wait(e, s_ma, A0 + 3 + lv)
                if lv < LEVELS - 1:
                    for m, i, h in ms:
                        ins = e.matmul(RB(2)[:, m * P:(m + 1) * P], U_[:, m, :], M1[:, m, :], start=True, stop=True)
                    ins.then_inc(s_mp, 1)
                for m, i, h in ms:
                    ins = e.matmul(RB(0)[:, m * P:(m + 1) * P], M1[:, m, :], U_[:, m, :], start=True, stop=True)
                ins.then_inc(s_mp, 1)
                yield
            wait(e, s_ul, (b + 1) * NUL)
            for m, i, h in ms:
                ins = e.matmul(RB(3)[:, m * P:(m + 1) * P], U_[:, m, :], RHS[:, m, :], start=True, stop=True)
            ins.then_inc(s_mp, 1)
            yield
            wait(e, s_ma, A0 + 9)
            for m, i, h in ms:
                e.matmul(RB(2)[h, i * P:(i + 1) * P], WY[:, m, 0:HD], AM[:, m, 1, :], start=True, stop=True)
            for m, i, h in ms:
                for c in range(2):
                    r = slice(c * C, (c + 1) * C)
                    ins = e.matmul(RB(2 - c)[h, 256 + i * C:256 + (i + 1) * C], WY[r, m, 0:HD],
                                   TOK[r, i, 1, h], start=True, stop=True)
            ins.then_inc(s_mp, 1)
            for m, i, h in ms:
                o = RB(0)[h, i * P:(i + 1) * P]
                e.matmul(o, WY[:, m, HD:P], AM[:, m, 1, :], start=True, stop=False)
                e.matmul(o, TOK[:, i, 0, h], AM[:, m, 3, :], start=False, stop=True)
            for m, i, h in ms:
                for c in range(2):
                    r = slice(c * C, (c + 1) * C)
                    o = RB(3 * c)[h, 256 + i * C:256 + (i + 1) * C]
                    e.matmul(o, TOK[r, i, 1, h], WY[r, m, HD:P], start=True, stop=False)
                    ins = e.matmul(o, TOK[r, i, 2, h], TOK[r, i, 0, h], start=False, stop=True)
            ins.then_inc(s_mp, 1)
            for c in range(4):
                yield
                wait(e, s_md, D0 + 5 + c)
                for hh in range(2):
                    h = slice(hh * HD, (hh + 1) * HD)
                    ins = e.matmul(RB(1)[h, c * C:(c + 1) * C], HF[h, 256 + c * C:256 + (c + 1) * C],
                                   ST[h, (4 * q + c) % 5, :], start=True, stop=True)
                ins.then_inc(s_mp, 1)
                if c == 0:
                    wait(e, s_ma, A0 + 10)
                for hh in range(2):
                    h = slice(hh * HD, (hh + 1) * HD)
                    ins = e.matmul(RB(3)[h, c * C:(c + 1) * C], ST[h, (4 * q + c) % 5, :],
                                   HF[h, c * C:(c + 1) * C], start=True, stop=True)
            ins.then_inc(s_mp, 1)

        def mats_act(e, b):
            g, q, ms = mats_of(b)
            P0, D0, A0 = b * MP, b * MD, b * MA
            for i in range(2):
                wait(e, s_mp, P0 + 5 + i)
                e.copy(RHS[:, 2 * i:2 * i + 2, 0:HD], RB(i)[:, 0:P].rearrange("p (h c) -> p h c", h=2))
                e.copy(TOK[:, i, :, :], RB(i)[:, P:4 * P].rearrange("p (k c) -> p k c", k=3)).then_inc(s_ma, 1)
            yield
            wait(e, s_mp, P0 + 8)
            e.copy(RHS[:, :, HD:P], RB(1)[:, 0:4 * HD].rearrange("p (m c) -> p m c", m=4)).then_inc(s_ma, 1)
            for lv in range(1, LEVELS):
                wait(e, s_mp, P0 + p_level(lv, 0))
                e.copy(M1[:, :, :], four(RB(3))).then_inc(s_ma, 1)
                yield
                yield
            wait(e, s_mp, P0 + P_T)
            e.mul(WY[:, :, :], four(RB(3)), -1.0).then_inc(s_ma, 1)
            yield
            wait(e, s_mp, P0 + P_JG)
            e.copy(JG[:, 0:256], RB(0)[:, 0:256])
            gc = JG[:, 256:512].rearrange("p (i c k) -> p i c k", i=2, c=2)
            for c in range(2):
                ins = e.copy(gc[:, :, c, :], RB(3 * c)[:, 256:384].rearrange("p (i k) -> p i k", i=2))
            ins.then_inc(s_ma, 1)
            for c in range(4):
                yield

        def mats_dve(e, b):
            g, q, ms = mats_of(b)
            P0, D0, A0 = b * MP, b * MD, b * MA

            def level(x, mask, lv, src):
                return e.copy_predicated(x[:, :, :], mask[:, lv:lv + 1, :].broadcast_to([P, 4, P]), src)
            for m in range(4):
                wait(e, s_mp, P0 + m + 1)
                e.tensor_tensor(AM[:, m, :, :], four(RB(m)), mask4[:, :, :], ALU.mult).then_inc(s_md, 1)
            wait(e, s_init, b + 1)
            wait(e, s_mp, P0 + 7)
            level(T_, lower, 0, four(RB(2))).then_inc(s_tl, 1)
            wait(e, s_md, D0 + 4)
            level(U_, upper, 0, AM[:, :, 0, :]).then_inc(s_ul, 1)
            yield
            for lv in range(1, LEVELS):
                yield
                if lv < LEVELS - 1:
                    wait(e, s_tl, b * NTL + lv)
                    wait(e, s_mp, P0 + p_level(lv, 1))
                    level(T_, lower, lv, four(RB(2))).then_inc(s_tl, 1)
                wait(e, s_ul, b * NUL + lv)
                wait(e, s_mp, P0 + p_level(lv, 2))
                level(U_, upper, lv, four(RB(0))).then_inc(s_ul, 1)
                yield
            yield
            wait(e, s_mp, P0 + P_HF)
            e.tensor_tensor(HF[:, 0:256], RB(2)[:, 0:256], RW[:, g, 256 * q:256 * q + 256], ALU.add)
            if q == 0:
                e.memset(ST[:, 0, :], 0.0)
            for c in range(4):
                ins = e.scalar_tensor_tensor(HF[:, 256 + c * C:256 + (c + 1) * C], ident2[:, :],
                                             pc[:, g, 4 * q + c:4 * q + c + 1],
                                             RB(2 - c % 2)[:, 256 + (c // 2) * C:256 + (c // 2 + 1) * C],
                                             ALU.mult, ALU.add)
            ins.then_inc(s_md, 1)
            yield
            wait(e, s_ma, A0 + 10)
            for c in range(4):
                wait(e, s_mp, P0 + P_ST + 1 + c)
                e.tensor_tensor(ST[:, (4 * q + c + 1) % 5, :], RB(1)[:, c * C:(c + 1) * C],
                                JG[:, 256 + c * C:256 + (c + 1) * C], ALU.add).then_inc(s_md, 1)
                if c < 3:
                    yield
            wait(e, s_mp, P0 + MP)
            e.tensor_tensor(KB[:, g, 256 * q:256 * q + 256], RB(3)[:, 0:256], JG[:, 0:256], ALU.add)\
                .then_inc(s_md, 1)

        def side_by_side(mats, piece, e, b):
            for k, _ in enumerate(mats(e, b)):
                if GAPS * b + k:
                    piece(e, GAPS * b + k - 1)

        def rnorm_pe(e, g):
            O = KB[:, g, :]
            wait(e, s_md, (g + 1) * NQ * MD)
            heads_sum(e, PS[2], O).then_inc(s_fp, 1)
            if g:
                snorm_pe(e, g - 1)
            wait(e, s_fd, 4 * g + 1)
            for half in range(2):
                ins = e.matmul(PS[2][:, half * HB:(half + 1) * HB], g_up[:, g * P:(g + 1) * P],
                               RW[:, 10, half * HB:(half + 1) * HB], start=True, stop=True)
            ins.then_inc(s_fp, 1)
            wait(e, s_fa, 3 * g + 1)
            heads_sum(e, PS[3], TT[:, 1, :]).then_inc(s_fp, 1)

        def rnorm_act(e, g):
            x = TT[:, 1, :]
            wait(e, s_fd, 4 * g + 1)
            e.activation(x, KB[:, g, :], ACT.Square).then_inc(s_fa, 1)
            wait(e, s_fp, 3 * g + 3)
            wait(e, s_fa, 3 * g + 1)
            e.activation(x, PS[3][:, :], ACT.Ln, scale=1.0 / HD, bias=consts[:, 2:3]).then_inc(s_fa, 1)
            wait(e, s_fa, 3 * g + 2)
            e.activation(x, x, ACT.Exp, scale=-0.5).then_inc(s_fa, 1)

        def rnorm_dve(e, g):
            O, Y = KB[:, g, :], YT[:, g, :]
            wait(e, s_md, (g + 1) * NQ * MD)
            wait(e, s_fp, 3 * g + 1)
            e.scalar_tensor_tensor(O, PS[2][:, :], -1.0 / HD, O, ALU.mult, ALU.add).then_inc(s_fd, 1)
            wait(e, s_fd, 4 * g + 1)
            wait(e, s_fa, 3 * g + 3)
            e.scalar_tensor_tensor(O, O, v1(V_LNG + g), TT[:, 1, :], ALU.mult, ALU.mult).then_inc(s_fd, 1)
            wait(e, s_fd, 4 * g + 2)
            e.scalar_tensor_tensor(Y, O, v1(V_LNB + g), Y, ALU.add, ALU.add).then_inc(s_fd, 1)
            wait(e, s_fd, 4 * g + 3)
            wait(e, s_fp, 3 * g + 2)
            e.tensor_tensor(Y, Y, PS[2][:, :], ALU.mult).then_inc(s_fd, 1)

        NU = NPAIR * NT * 2
        Rl = TT[:, 0, :]

        def unit(u):
            g, n, hh = u // (2 * NT), (u // 2) % NT, u % 2
            i = n // 2 if n % 2 == 0 else NT - 1 - n // 2
            return g, i, hh, slice(hh * HD, (hh + 1) * HD), (i + 1) * P, 1 + (i > 0)

        def group(i, k):
            cut = max(1, (i + 1) // 2)
            return (0, cut) if k == 0 else (cut, i + 1)

        def groups(u):
            return sum(unit(x)[5] for x in range(u))
        BD, BA = 3, 4

        GAPS = 16

        def sba_pe(e, j):
            u, kind = j // 4, j % 4
            if kind == 0:
                if u == NU:
                    return
                g, i, hh, h, kv, ng = unit(u)
                wait(e, s_pe, LRU_T + SBA_T + NT)
                wait(e, s_bd, BD * u)
                if u % (2 * NT) == 0 and g >= 2:
                    wait(e, s_na, 3 * (g - 2) + 2)
                for lo in range(0, kv, HB):
                    hi = min(kv, lo + HB)
                    last = hi == kv
                    ins = e.matmul(PS[0][:, lo:hi], SQ[h, g, i * P:(i + 1) * P], SQ[h, 3 + g, lo:hi],
                                   start=True, stop=not last)
                ins = e.matmul(PS[0][:, kv - P:kv], identb[:, :], causal_neg[:, :], start=False, stop=True)
                ins.then_inc(s_bz, 1)
                return
            u -= 1
            if u < 0:
                return
            g, i, hh, h, kv, ng = unit(u)
            if kind <= ng:
                k = kind - 1
                wait(e, s_ba, BA * u + 4)
                wait(e, s_bt, groups(u) + k)
                lo, hi = group(i, k)
                for st in range(lo, hi):
                    ins = e.transpose(PS[1][:, (st - lo) * P:(st - lo + 1) * P], Eb[u % 2][:, st * P:(st + 1) * P],
                                      ident[:, :])
                ins.then_inc(s_bx, 1)
            if kind == 3:
                wait(e, s_bt, groups(u + 1))
                if hh == 0:
                    wait(e, s_bo, u // 2)
                for st in range(i + 1):
                    ins = e.matmul(PS[1][h, HB + (i % 4) * P:HB + (i % 4 + 1) * P],
                                   SV[:, st, g * P + hh * HD:g * P + (hh + 1) * HD],
                                   ATb[u % 2][:, st * P:(st + 1) * P], start=st == 0, stop=st == i)
                ins.then_inc(s_bv, 1)

        def sba_act(e, j):
            u, kind = j // 4, j % 4
            if kind == 0:
                if 1 <= u <= NU:
                    E_ = Eb[(u - 1) % 2][:, 0:unit(u - 1)[4]]
                    wait(e, s_bd, BD * u)
                    e.activation(E_, E_, ACT.Exp).then_inc(s_ba, 1)
                if u >= 2 and u % 2 == 1:
                    g, i, hh, h, kv, ng = unit(u - 2)
                    wait(e, s_bv, u - 1)
                    e.copy(YT[:, 5 + g, i * P:(i + 1) * P], PS[1][:, HB + (i % 4) * P:HB + (i % 4 + 1) * P])\
                     .then_inc(s_bo, 1)
                if u >= NU:
                    return
                kv = unit(u)[4]
                E_ = Eb[u % 2][:, 0:kv]
                wait(e, s_bz, u + 1)
                if u == 0:
                    wait(e, s_pp, CT + NT)
                wait(e, s_bx, groups(u - 1) if u > 1 else 0)
                e.activation(E_, PS[0][:, 0:kv], ACT.Abs).then_inc(s_ba, 1)
                e.wait_ge(s_ba, BA * u + 1)
                e.activation(E_, E_, ACT.Exp, scale=-1.0).then_inc(s_ba, 1)
                e.wait_ge(s_ba, BA * u + 2)
                e.activation(E_, E_, ACT.Ln, bias=1.0).then_inc(s_ba, 1)

        def sba_scan(e, u):
            kv = unit(u)[4]
            E_, R_ = Eb[u % 2][:, 0:kv], Rl[:, 0:kv]
            wait(e, s_ba, BA * u + 3)
            wait(e, s_bd, BD * u + 1)
            e.tensor_tensor_scan(R_[:, ::-1], E_[:, ::-1], R_[:, ::-1], 0.0, ALU.add, ALU.add).then_inc(s_bd, 1)
            wait(e, s_bd, BD * u + 2)
            e.tensor_tensor(E_, PS[0][:, 0:kv], R_, ALU.subtract).then_inc(s_bd, 1)

        def sba_dve(e, j):
            u, kind = j // 4, j % 4
            if kind in (1, 2) and u >= 1 and kind <= unit(u - 1)[5]:
                v, k = u - 1, kind - 1
                i = unit(v)[1]
                wait(e, s_bx, groups(v) + k + 1)
                wait(e, s_bv, v - 1)
                lo, hi = group(i, k)
                e.tensor_copy(ATb[v % 2][:, lo * P:hi * P], PS[1][:, 0:(hi - lo) * P]).then_inc(s_bt, 1)
            if u == NU:
                return
            if kind == 1:
                kv = unit(u)[4]
                wait(e, s_bz, u + 1)
                wait(e, s_bd, BD * u)
                wait(e, s_ba, BA * u + 1)
                e.tensor_scalar_max(Rl[:, 0:kv], PS[0][:, 0:kv], 0.0).then_inc(s_bd, 1)
            if kind == 3 and u % 4 < 3:
                sba_scan(e, u)

        def snorm_act(e, g):
            x = TT[:, 2, :]
            wait(e, s_bo, NT * (g + 1))
            wait(e, s_nd, g)
            e.activation(x, YT[:, 5 + g, :], ACT.Square).then_inc(s_na, 1)
            wait(e, s_np, g + 1)
            wait(e, s_na, 3 * g + 1)
            e.activation(x, PS[0][:, :], ACT.Ln, scale=1.0 / HD, bias=consts[:, 0:1]).then_inc(s_na, 1)
            wait(e, s_na, 3 * g + 2)
            e.activation(x, x, ACT.Exp, scale=-0.5).then_inc(s_na, 1)

        def snorm_pe(e, g):
            wait(e, s_na, 3 * g + 1)
            wait(e, s_bd, BD * 2 * NT * min(g + 2, NPAIR))
            heads_sum(e, PS[0], TT[:, 2, :]).then_inc(s_np, 1)

        def snorm_dve(e, g):
            wait(e, s_na, 3 * g + 3)
            e.scalar_tensor_tensor(YT[:, 5 + g, :], YT[:, 5 + g, :], v1(V_SG + g), TT[:, 2, :], ALU.mult, ALU.mult)\
                .then_inc(s_nd, 1)

        WO = [RW[:, 0, :], RW[:, 3, :], RW[:, 6, :], RW[:, 1, :], RW[:, 4, :], RW[:, 7, :], KB[:, 3, :], KB[:, 4, :]]
        XR = [KB[:, 0, :], KB[:, 1, :], KB[:, 2, :], KB[:, 5, :]]
        LN1 = [RW[:, 2, :], RW[:, 5, :]]
        LN2 = [TT[:, 1, :], TT[:, 2, :]]
        X1 = SQ[:, 0:NT, :]
        X1T = TT[:, 0, :]
        RX = RW[:, 8:11, :].rearrange("p a b -> p (a b)")
        roff = [0]

        def small(n):
            a = roff[0]
            roff[0] += n
            return RX[:, a:a + n]
        before, ones = small(P), small(P)
        rt_w = small(KT * E_N)
        rt_b = small(E_N)
        stats, mv = small(2 * 12).rearrange("p (b c) -> p b c", b=2), small(2 * 4).rearrange("p (b c) -> p b c", b=2)
        slot = small(2 * NT).bitcast(U32).rearrange("p (k i) -> p k i", k=2)
        gate = small(2 * NT).rearrange("p (k i) -> p k i", k=2)
        tab = small(64).bitcast(I32)
        blk_iota = small((MAXB + 1) * E_N)
        rev4, rev16 = small(G_E), small(E_N)
        NORM_D, NORM_A = 6, 3

        def norm_dve(e, i, sd, sa, x, res, g, b, d0, a0):
            st, m = stats[:, i % 2, :], mv[:, i % 2, :]
            for half in range(2):
                ins = e.bn_stats(st[:, 6 * half:6 * half + 6], x[:, half * HB:(half + 1) * HB])
            ins.then_inc(sd, 1)
            wait(e, sd, d0 + 1)
            e.bn_aggr(m[:, 0:2], st).then_inc(sd, 1)
            wait(e, sd, d0 + 2)
            wait(e, sa, a0 + 2)
            e.scalar_tensor_tensor(m[:, 3:4], m[:, 0:1], -1.0, m[:, 2:3], ALU.mult, ALU.mult).then_inc(sd, 1)
            wait(e, sa, a0 + 3)
            e.tensor_tensor(x, x, g, ALU.mult).then_inc(sd, 1)
            wait(e, sd, d0 + 4)
            e.tensor_tensor(res, x, b, ALU.add).then_inc(sd, 1)

        def norm_act(e, i, sd, sa, x, d0, a0):
            m = mv[:, i % 2, :]
            wait(e, sa, a0)
            wait(e, sd, d0 + 2)
            e.activation(m[:, 2:3], m[:, 1:2], ACT.Ln, bias=consts[:, 3:4]).then_inc(sa, 1)
            wait(e, sa, a0 + 1)
            e.activation(m[:, 2:3], m[:, 2:3], ACT.Exp, scale=-0.5).then_inc(sa, 1)
            wait(e, sd, d0 + 3)
            wait(e, sa, a0 + 2)
            e.activation(x, x, ACT.Identity, scale=m[:, 2:3], bias=m[:, 3:4]).then_inc(sa, 1)

        def mixed_sp(e):
            wait(e, s_fd, 4 * 2)
            for kt in range(KT):
                e.dma_start(WO[kt], t["w_out"][kt]).then_inc(s_wo, 16)
            wait(e, s_fd, 4 * NPAIR)
            for k in range(2):
                e.dma_start(LN1[k], t["ln"][k:k + 1, :].broadcast_to([P, D])).then_inc(s_rc, 16)
            e.dma_start(rt_w, t["router_w"]).then_inc(s_rc, 16)
            e.dma_start(rt_b, t["router_b"].broadcast_to([P, E_N])).then_inc(s_rc, 16)
            for i in range(NT):
                if i >= 4:
                    wait(e, s_n1d, NORM_D * (i - 3))
                if i == 3:
                    wait(e, s_mp, NB * MP)
                e.dma_start(XR[i % 4], t["x"][i * P:(i + 1) * P, :]).then_inc(s_xr[i % 4], 16)

        def out_pe(e, i):
            if i == 0:
                wait(e, s_fd, 4 * NPAIR)
                wait(e, s_nd, NPAIR)
                wait(e, s_wo, 16 * KT)
            if i >= 2:
                wait(e, s_n1d, NORM_D * (i - 2) + 1)
            for half in range(2):
                for kt in range(KT):
                    ins = e.matmul(PS[i % 2][:, half * HB:(half + 1) * HB], YT[:, kt, i * P:(i + 1) * P],
                                   WO[kt][:, half * HB:(half + 1) * HB], start=kt == 0, stop=kt == KT - 1)
            ins.then_inc(s_op, 1)

        def out_dve(e, i):
            d0 = NORM_D * i
            x = XR[i % 4]
            if i == 0:
                wait(e, s_rc, 16 * 4)
            wait(e, s_op, i + 1)
            wait(e, s_xr[i % 4], 16 * (i // 4 + 1))
            e.scalar_tensor_tensor(x, x, ALPHA, PS[i % 2][:, :], ALU.mult, ALU.add).then_inc(s_n1d, 1)
            wait(e, s_n1d, d0 + 1)
            norm_dve(e, i, s_n1d, s_n1a, x, X1[:, i, :], LN1[0], LN1[1], d0 + 1, NORM_A * i)

        def logits_pe(e, i):
            wait(e, s_n1d, NORM_D * (i + 1))
            wait(e, s_x1t, i)
            for kt in range(KT):
                ins = e.transpose(PS[2][:, kt * P:(kt + 1) * P], X1[:, i, kt * P:(kt + 1) * P], ident[:, :])
            ins.then_inc(s_x1p, 1)
            wait(e, s_x1t, i + 1)
            for kt in range(KT):
                ins = e.matmul(PS[3][:, i * E_N:(i + 1) * E_N], X1T[:, kt * P:(kt + 1) * P],
                               rt_w[:, kt * E_N:(kt + 1) * E_N], start=kt == 0, stop=kt == KT - 1)
            ins.then_inc(s_lg, 1)

        def logits_act(e, i):
            wait(e, s_x1p, i + 1)
            wait(e, s_lg, i)
            e.copy(X1T, PS[2][:, :]).then_inc(s_x1t, 1)

        lg, pr, pm, k16, oh1, oh2, am, pos = [small(NT * E_N) for _ in range(8)]
        q1, q2, q3, g4, k4 = [small(NT * E_G) for _ in range(5)]
        c8 = [small(NT) for _ in range(3)]
        base = small((NT + 1) * E_N)
        first, last, nblk, b_end, b_sta, b_off, zero = [small(E_N) for _ in range(7)]
        assert roff[0] <= 3 * S

        def te(x):
            return x.rearrange("p (i e) -> p i e", e=E_N)

        def over(x, n):
            return x.rearrange("p (m o) -> p m o", o=1).broadcast_to([P, x.shape[1], n])

        def under(x, n):
            return x.rearrange("p (o m) -> p o m", o=1).broadcast_to([P, n, x.shape[1]])

        def router_pool(e):
            wait(e, s_fd, 4 * NPAIR)
            e.memset(ones, 1.0)
            e.memset(zero, 0.0)
            e.iota(rev4, [[-1, G_E]], base=G_E, channel_multiplier=0, allow_small_or_imprecise_dtypes=True)
            e.iota(rev16, [[-1, E_N]], base=E_N, channel_multiplier=0, allow_small_or_imprecise_dtypes=True)
            e.iota(blk_iota, [[1, MAXB + 1], [0, E_N]], base=0, channel_multiplier=0,
                   allow_small_or_imprecise_dtypes=True).then_inc(s_rpool, 1)
            e.wait_ge(s_rpool, 1)
            e.affine_select(out=before, in_=ones, compare_op=ALU.is_gt, fill=0.0, base=0,
                            pattern=[[1, P]], channel_multiplier=-1).then_inc(s_rpool, 1)

        def router_dve(e):
            n = [0]

            def step(ins):
                ins.then_inc(s_q, 1)
                n[0] += 1
                e.wait_ge(s_q, n[0])
            TTo, RED = e.tensor_tensor, e.tensor_reduce
            wait(e, s_lg, NT)
            wait(e, s_rpool, 2)
            step(TTo(te(lg), te(PS[3][:, 0:NT * E_N]), under(rt_b, NT), ALU.add))
            step(RED(c8[0], te(lg), AX.X, ALU.max))
            TTo(te(lg), te(lg), over(c8[0], E_N), ALU.subtract).then_inc(s_qd, 1)
            e.wait_ge(s_qa, 1)
            step(RED(c8[0], te(pr), AX.X, ALU.add))
            step(e.reciprocal(c8[1], c8[0]))
            step(TTo(te(pr), te(pr), over(c8[1], E_N), ALU.mult))
            step(RED(q1, pr.rearrange("p (q e) -> p q e", e=G_E), AX.X, ALU.max))
            quad = lambda x: x.rearrange("p (q e) -> p q e", e=G_E)
            step(TTo(quad(k16), quad(pr), over(q1, G_E), ALU.is_equal))
            step(TTo(quad(k16), quad(k16), under(rev4, NT * E_G), ALU.mult))
            step(RED(q2, quad(k16), AX.X, ALU.max))
            step(TTo(quad(k16), quad(k16), over(q2, G_E), ALU.is_equal))
            step(e.scalar_tensor_tensor(pm, k16, -2.0, pr, ALU.mult, ALU.add))
            step(RED(q2, quad(pm), AX.X, ALU.max))
            step(TTo(q1, q1, q2, ALU.add))
            step(RED(c8[0], quad(q1), AX.X, ALU.max))
            step(TTo(quad(g4), quad(q1), over(c8[0], E_G), ALU.is_equal))
            step(TTo(quad(g4), quad(g4), under(rev4, NT), ALU.mult))
            step(RED(c8[1], quad(g4), AX.X, ALU.max))
            step(TTo(quad(g4), quad(g4), over(c8[1], E_G), ALU.is_equal))
            step(TTo(quad(pm), quad(pr), over(g4, G_E), ALU.mult))
            step(e.tensor_scalar_add(k4, g4, -1.0))
            step(TTo(quad(pm), quad(pm), over(k4, G_E), ALU.add))
            for k, oh in enumerate((oh1, oh2)):
                step(RED(c8[k], te(pm), AX.X, ALU.max))
                step(TTo(te(k16), te(pm), over(c8[k], E_N), ALU.is_equal))
                step(TTo(te(k16), te(k16), under(rev16, NT), ALU.mult))
                step(RED(c8[2], te(k16), AX.X, ALU.max))
                step(TTo(te(oh), te(k16), over(c8[2], E_N), ALU.is_equal))
                if k == 0:
                    step(e.scalar_tensor_tensor(pm, oh, -4.0, pm, ALU.mult, ALU.add))
            step(TTo(am, oh1, oh2, ALU.add))
            wait(e, s_q, n[0])
            e.memset(base[:, 0:E_N], 0.0).then_inc(s_qd, 1)
            step(TTo(c8[2], c8[0], c8[1], ALU.add))
            step(e.reciprocal(c8[2], c8[2]))
            for k in range(2):
                step(TTo(gate[:, k, :], c8[k], c8[2], ALU.mult))
            e.wait_ge(s_qp, 1)
            for i in range(NT):
                step(TTo(base[:, (i + 1) * E_N:(i + 2) * E_N], base[:, i * E_N:(i + 1) * E_N],
                         PS[2][:, i * E_N:(i + 1) * E_N], ALU.add))
            count = base[:, NT * E_N:]
            step(e.tensor_tensor_scan(last, count, zero, 0.0, ALU.add, ALU.add))
            step(TTo(first, last, count, ALU.subtract))
            step(TTo(pos, PS[3][:, 0:NT * E_N], base[:, 0:NT * E_N], ALU.add))
            step(TTo(te(pos), te(pos), under(first, NT), ALU.add))
            for k, oh in enumerate((oh1, oh2)):
                step(TTo(k16, pos, oh, ALU.mult))
                step(RED(c8[k], te(k16), AX.X, ALU.add))
                ins = e.tensor_copy(slot[:, k, :], c8[k])
                ins.then_inc(s_slot, 1)
            step(e.memset(nblk, 1.0))
            for j in range(1, NT):
                step(e.scalar_tensor_tensor(nblk, count, float(P * j), nblk, ALU.is_gt, ALU.add))
            step(e.tensor_tensor_scan(b_end, nblk, zero, 0.0, ALU.add, ALU.add))
            step(TTo(b_sta, b_end, nblk, ALU.subtract))
            step(e.scalar_tensor_tensor(b_off, b_sta, float(-P), first, ALU.mult, ALU.add))
            step(e.tensor_copy(tab[:, 0:E_N], b_sta))
            step(e.tensor_copy(tab[:, E_N:E_N + 1], b_end[:, E_N - 1:E_N]))
            W = MAXB + 1
            z1, z2 = XR[0][:, 0:W * E_N], XR[1][:, 0:W * E_N]
            r1 = XR[2][:, 0:W]
            step(TTo(te(z1), te(blk_iota), under(b_sta, W), ALU.is_ge))
            step(TTo(te(z2), te(blk_iota), under(b_end, W), ALU.is_lt))
            step(TTo(z1, z1, z2, ALU.mult))
            step(TTo(te(z1), te(z1), under(b_off, W), ALU.mult))
            step(RED(r1, te(z1), AX.X, ALU.add))
            step(e.scalar_tensor_tensor(r1, te(blk_iota)[:, :, 0], float(P), r1, ALU.mult, ALU.add))
            step(e.tensor_scalar_min(r1, r1, float(ROWS - P)))
            e.tensor_copy(tab[:, 20:20 + W], r1).then_inc(s_tab, 1)

        def router_act(e):
            e.wait_ge(s_qd, 1)
            e.activation(pr, lg, ACT.Exp).then_inc(s_qa, 1)

        def router_pe(e):
            e.wait_ge(s_qd, 2)
            e.matmul(PS[2][:, 0:NT * E_N], ones, am, start=True, stop=True)
            e.matmul(PS[3][:, 0:NT * E_N], before, am, start=True, stop=True).then_inc(s_qp, 1)

        xs = nc.dram_tensor("xs", (ROWS, D), F32).ap()
        ys = nc.dram_tensor("ys", (ROWS, D), F32).ap()
        XSf = XS[:, :, :].rearrange("p a b -> p (a b)")
        RWf, KBf = RW[:, :, :].rearrange("p a b -> p (a b)"), KB[:, :, :].rearrange("p a b -> p (a b)")
        WSET = [[XSf[:, 0:4 * S], XSf[:, 4 * S:8 * S], XSf[:, 8 * S:12 * S]],
                [RWf[:, 0:4 * S], RWf[:, 4 * S:8 * S], KBf[:, 0:4 * S]]]
        Xg, XgT, Yb = YT[:, 0, :], YT[:, 1, :], YT[:, 4, :]
        Sg, Hh, HhT = YT[:, 2, 0:HB], YT[:, 2, HB:2 * HB], YT[:, 3, 0:HB]

        def load_expert(e, x, k):
            pick = (lambda w: w[x]) if isinstance(x, int) else (lambda w: w[bass.ds(x, 1)].rearrange("o a b -> (o a) b"))
            for j, name in enumerate(("w_gate", "w_upx", "w_down")):
                n = E_F if j < 2 else D
                e.dma_start(WSET[k][j].rearrange("p (a f) -> p a f", f=n),
                            pick(t[name]).rearrange("(a p) f -> p a f", p=P))\
                 .then_inc((s_wg, s_wu, s_wd)[j][k], 16)

        def table(e, at, hi, lo=0):
            return e.value_load(tab[0:1, bass.ds(at, 1)] if not isinstance(at, int) else tab[0:1, at:at + 1],
                                min_val=lo, max_val=hi)

        def expert_blocks(e, body, pairs=(0, E_N // 2), after=None):
            with e.Fori(*pairs) as ep:
                for k in range(2):
                    b0 = table(e, 2 * ep + k, MAXB)
                    b1 = table(e, 2 * ep + k + 1, MAXB, 1)
                    with e.Fori(b0, b1) as i:
                        body(i, k, ep)
                    if after is not None:
                        after(ep, k)

        def ahead(e, *sems):
            for x in sems:
                e.sem_inc(x)

        def moe_sp(e):
            ahead(e, s_ys)
            wait(e, s_mp, NB * MP)
            wait(e, s_bv, NU)
            wait(e, s_md, NB * MD)
            load_expert(e, 0, 0)
            wait(e, s_op, NT)
            wait(e, s_tab, 1)
            load_expert(e, 1, 1)
            for k in range(2):
                e.dma_start(LN2[k], t["ln"][2 + k:3 + k, :].broadcast_to([P, D])).then_inc(s_l2, 16)

            def store(i, k, ep):
                row = table(e, 20 + i, ROWS - P)
                e.wait_ge(s_ya, i + 2)
                e.wait_ge(s_yd, i + 2)
                e.sem_inc(s_tick[0])
                e.wait_ge(s_ys, i * 16 + 1)
                e.sem_inc(s_tick[0])
                e.dma_start(ys[bass.ds(row, P)], Yb).then_inc(s_ys, 16)
            expert_blocks(e, store, (0, E_N // 2 - 1), lambda ep, k: load_expert(e, 2 * ep + 2 + k, k))
            expert_blocks(e, store, (E_N // 2 - 1, E_N // 2))

        def moe_pool(e):
            wait(e, s_n1d, NORM_D * NT)
            e.dma_start(xs[2 * S:ROWS], X1[:, 0, :]).then_inc(s_sc, 16)
            for k in range(2):
                wait(e, s_slot, k + 1)
                for i in range(NT):
                    e.indirect_dma_start(xs, bass.IndirectOffsetOnAxis(slot[:, k, i:i + 1], 0), X1[:, i, :], None)\
                     .then_inc(s_sc, 16)
            e.wait_ge(s_sc, 16 * (2 * NT + 1))
            wait(e, s_tab, 1)
            total = table(e, E_N, MAXB, E_N)
            with e.Fori(0, total + 1) as i:
                row = table(e, 20 + i, ROWS - P)
                e.wait_ge(s_xgp, i + 1)
                e.dma_start(Xg, xs[bass.ds(row, P)]).then_inc(s_xg, 16)
            e.wait_ge(s_ys, total * 16 + 1)
            e.sem_inc(s_tick[1])
            for i in range(NT):
                for k in range(2):
                    n = 2 * i + k
                    if n >= 12:
                        wait(e, s_n2d, N2_D * ((n - 12) // 2) + 1 + k)
                    e.indirect_dma_start(XS[:, n % 12, :], None, ys[0:2 * S, :], bass.IndirectOffsetOnAxis(slot[:, k, i:i + 1], 0))\
                     .then_inc(s_gt[n % 12], 16)

        def xg_transposes(e):
            for kt in range(KT):
                ins = e.transpose(PS[1][:, kt * P:(kt + 1) * P], Xg[:, kt * P:(kt + 1) * P], ident[:, :])
            ins.then_inc(s_xgp, 1)

        def moe_pe(e):
            ahead(e, s_xgp, s_htp, s_y1)
            e.wait_ge(s_xg, 16)
            xg_transposes(e)

            def body(i, k, ep):
                wg, wu, wd = WSET[k]
                e.wait_ge(s_wg[k], 16 * (ep + 1))
                e.wait_ge(s_ta, i + 1)
                e.wait_ge(s_td, i + 1)
                e.wait_ge(s_hd, i + 1)
                for kt in range(KT):
                    ins = e.matmul(PS[0][:, 0:HB], XgT[:, kt * P:(kt + 1) * P], wg[:, kt * E_F:(kt + 1) * E_F],
                                   start=kt == 0, stop=kt == KT - 1)
                ins.then_inc(s_g1, 1)
                e.wait_ge(s_wu[k], 16 * (ep + 1))
                for kt in range(KT):
                    ins = e.matmul(PS[0][:, HB:2 * HB], XgT[:, kt * P:(kt + 1) * P], wu[:, kt * E_F:(kt + 1) * E_F],
                                   start=kt == 0, stop=kt == KT - 1)
                ins.then_inc(s_u1, 1)
                e.wait_ge(s_xg, 16 * (i + 2))
                xg_transposes(e)
                e.wait_ge(s_hd, i + 2)
                e.wait_ge(s_htd, i + 1)
                for f in range(FT):
                    ins = e.transpose(PS[2][:, f * P:(f + 1) * P], Hh[:, f * P:(f + 1) * P], ident[:, :])
                ins.then_inc(s_htp, 1)
                e.wait_ge(s_wd[k], 16 * (ep + 1))
                e.wait_ge(s_htd, i + 2)
                e.wait_ge(s_ya, i + 1)
                e.wait_ge(s_yd, i + 1)
                for half in range(2):
                    for f in range(FT):
                        ins = e.matmul(PS[3][:, half * HB:(half + 1) * HB], HhT[:, f * P:(f + 1) * P],
                                       wd[:, f * D + half * HB:f * D + (half + 1) * HB], start=f == 0, stop=f == FT - 1)
                ins.then_inc(s_y1, 1)
            expert_blocks(e, body)

        def moe_act(e):
            ahead(e, s_ya)
            e.wait_ge(s_xgp, 2)
            e.copy(XgT[:, 0:HB], PS[1][:, 0:HB]).then_inc(s_ta, 1)

            def body(i, k, ep):
                e.wait_ge(s_g1, i + 1)
                e.wait_ge(s_hd, i + 1)
                e.activation(Sg, PS[0][:, 0:HB], ACT.Silu).then_inc(s_si, 1)
                e.wait_ge(s_xgp, i + 3)
                e.copy(XgT[:, 0:HB], PS[1][:, 0:HB]).then_inc(s_ta, 1)
                e.wait_ge(s_y1, i + 2)
                e.wait_ge(s_ys, i * 16 + 1)
                e.copy(Yb[:, 0:HB], PS[3][:, 0:HB]).then_inc(s_ya, 1)
            expert_blocks(e, body)

        def moe_dve(e):
            ahead(e, s_hd, s_yd, s_htd)
            e.wait_ge(s_xgp, 2)
            e.tensor_copy(XgT[:, HB:2 * HB], PS[1][:, HB:2 * HB]).then_inc(s_td, 1)

            def body(i, k, ep):
                e.wait_ge(s_u1, i + 1)
                e.wait_ge(s_si, i + 1)
                e.wait_ge(s_htp, i + 1)
                e.tensor_tensor(Hh, Sg, PS[0][:, HB:2 * HB], ALU.mult).then_inc(s_hd, 1)
                e.wait_ge(s_xgp, i + 3)
                e.tensor_copy(XgT[:, HB:2 * HB], PS[1][:, HB:2 * HB]).then_inc(s_td, 1)
                e.wait_ge(s_htp, i + 2)
                e.wait_ge(s_y1, i + 1)
                e.tensor_copy(HhT, PS[2][:, 0:HB]).then_inc(s_htd, 1)
                e.wait_ge(s_y1, i + 2)
                e.wait_ge(s_ys, i * 16 + 1)
                e.tensor_copy(Yb[:, HB:2 * HB], PS[3][:, HB:2 * HB]).then_inc(s_yd, 1)
            expert_blocks(e, body)

        N2_D, N2_A = 7, 4

        def final_dve(e, i):
            d0, a0 = N2_D * i, N2_A * i
            x = X1[:, i, :]
            if i == 0:
                wait(e, s_l2, 32)
            wait(e, s_n2a, a0 + 1)
            for k in range(2):
                n = 2 * i + k
                wait(e, s_gt[n % 12], 16 * (n // 12 + 1))
                wait(e, s_n2d, d0 + k)
                e.scalar_tensor_tensor(x, XS[:, n % 12, :], gate[:, k, i:i + 1], x, ALU.mult, ALU.add).then_inc(s_n2d, 1)
            wait(e, s_n2d, d0 + 2)
            norm_dve(e, i, s_n2d, s_n2a, x, x, LN2[0], LN2[1], d0 + 2, a0 + 1)

        def final_act(e, i):
            d0, a0 = N2_D * i, N2_A * i
            if i == 0:
                e.wait_ge(s_sc, 16 * (2 * NT + 1))
            wait(e, s_n2a, a0)
            e.mul(X1[:, i, :], X1[:, i, :], ALPHA).then_inc(s_n2a, 1)
            norm_act(e, i, s_n2d, s_n2a, X1[:, i, :], d0 + 2, a0 + 1)

        def final_sp(e):
            for i in range(NT):
                wait(e, s_n2d, N2_D * (i + 1))
                e.dma_start(out[0, i * P:(i + 1) * P, :], X1[:, i, :]).then_inc(s_out, 16)
            e.wait_ge(s_out, 16 * NT)

        @block.sync
        def _(e):
            proj_sp(e)
            mixed_sp(e)
            moe_sp(e)
            final_sp(e)

        @block.gpsimd
        def _(e):
            masks_pool(e)
            mats_pool(e)
            router_pool(e)
            moe_pool(e)

        @block.scalar
        def _(e):
            lam_act(e)
            for n in range(CT + NT):
                proj_act(e, n)
                if n == 14:
                    lru_act(e, 0, 0)
                if n == 15:
                    lru_act(e, 0, 1)
                if n == 16:
                    lru_act(e, 1, 0)
                if n == 17:
                    lru_act(e, 1, 1)
                if n == 18:
                    rw_pre_act(e)
                    rw_act(e, 0, 0)
                if n == 19:
                    rw_act(e, 0, 1)
                if n == 20:
                    rw_act(e, 1, 0)
                if n == 21:
                    rw_act(e, 1, 1)
                if n == 23:
                    rw_act(e, 2, 0)
                if n == 24:
                    rw_act(e, 2, 1)
            for b in range(NB):
                side_by_side(mats_act, sba_act, e, b)
                if b % NQ == NQ - 1:
                    if b // NQ:
                        snorm_act(e, b // NQ - 1)
                    rnorm_act(e, b // NQ)
            for j in range(4 * NU - 1, 4 * NU + 5):
                sba_act(e, j)
            snorm_act(e, NPAIR - 1)
            for i in range(NT):
                norm_act(e, i, s_n1d, s_n1a, XR[i % 4], NORM_D * i + 1, NORM_A * i)
                if i >= 1:
                    logits_act(e, i - 1)
            logits_act(e, NT - 1)
            router_act(e)
            moe_act(e)
            exp_ln(e)
            for i in range(NT):
                final_act(e, i)

        @block.vector
        def _(e):
            masks_dve(e)
            for n in range(RW_T):
                proj_dve(e, n)
            for u in range(2):
                lru_dve(e, u)
            for g in range(NPAIR):
                rw_dve(e, g)
            for b in range(NB):
                side_by_side(mats_dve, sba_dve, e, b)
                sba_scan(e, 4 * b + 3)
                if b % NQ == NQ - 1:
                    rnorm_dve(e, b // NQ)
                    if b // NQ:
                        snorm_dve(e, b // NQ - 1)
            for j in range(4 * NU - 1, 4 * NU + 4):
                sba_dve(e, j)
            snorm_dve(e, NPAIR - 1)
            for i in range(NT):
                out_dve(e, i)
            router_dve(e)
            moe_dve(e)
            for i in range(NT):
                final_dve(e, i)

        @block.tensor
        def _(e):
            after = {15: (lru_pe, 0, 0), 16: (lru_pe, 0, 2), 17: (lru_pe, 1, 0), 18: (lru_pe, 1, 2),
                     19: (rw_pe, 0, 0), 20: (rw_pe, 0, 1), 21: (rw_pe, 0, 2), 22: (rw_pe, 1, 0), 23: (rw_pe, 1, 1),
                     24: (rw_pe, 1, 2), 25: (rw_pe, 2, 0), 26: (rw_pe, 2, 1), 27: (rw_pe, 2, 2)}
            for n in range(CT + NT):
                proj_pe(e, n)
                if n in after:
                    f, u, part = after[n]
                    f(e, u, part)
                    if f is lru_pe and part == 0:
                        lru_pe(e, u, 1)
            for b in range(NB):
                side_by_side(mats_pe, sba_pe, e, b)
                if b % NQ == NQ - 1:
                    rnorm_pe(e, b // NQ)
            for j in range(4 * NU - 1, 4 * NU + 4):
                sba_pe(e, j)
            snorm_pe(e, NPAIR - 1)
            for i in range(NT):
                out_pe(e, i)
                if i >= 2:
                    logits_pe(e, i - 2)
            logits_pe(e, NT - 2)
            logits_pe(e, NT - 1)
            router_pe(e)
            moe_pe(e)


def lay_out(inputs, np):
    f = {k: np.asarray(v) for k, v in inputs.items()}
    tiles = lambda a: a.reshape(-1, P).T
    vecs = [tiles(f[k]) for k in ("shift_mu", "rwkv_w0", "rwkv_a0", "rwkv_k_k", "rwkv_k_a", "rwkv_r_k", "rwkv_ln_g",
                                  "rwkv_ln_b", "sba_norm_g", "lru_conv_w", "lru_conv_b", "lru_ba", "lru_bx",
                                  "lru_lambda", "lru_norm_g")]
    w = f["w_in"][0].reshape(KT, P, IN_COLS)
    lru = np.stack([f[k][0].reshape(2, 2, HD, HD) for k in ("lru_wa", "lru_wx")])
    a = {
        "x": f["x"][0],
        "xT": f["x"][0].T.reshape(KT, P, S),
        "w_in": w[:, :, :V_COL].reshape(KT, P, CT, P).transpose(2, 1, 0, 3).reshape(CT, P, D),
        "w_v": w[:, :, V_COL:].transpose(1, 0, 2).reshape(P, KT * SBA_W),
        "vecs": np.concatenate(vecs, axis=1),
        "lora_up": np.concatenate([f["rwkv_w_up"][0], f["rwkv_a_up"][0]], axis=0),
        "g_up": f["rwkv_g_up"][0],
        "lru_w": lru.transpose(2, 3, 0, 1, 4).reshape(P, 2, 2, HD),
        "w_out": f["w_out"][0].reshape(KT, P, D),
        "ln": np.stack([f[k][0] for k in ("ln1_g", "ln1_b", "ln2_g", "ln2_b")]),
        "router_w": f["router_w"].reshape(KT, P, E_N).transpose(1, 0, 2).reshape(P, KT * E_N),
        "router_b": f["router_b"].reshape(1, E_N),
        "w_gate": f["exp_w_gate"][0],
        "w_upx": f["exp_w_up"][0],
        "w_down": f["exp_w_down"][0],
    }
    return {k: np.ascontiguousarray(v) for k, v in a.items()}


def kernel(**inputs):
    import numpy as np
    import concourse.bacc as bacc
    from concourse.bass_utils import run_bass_kernel_spmd

    nc = bacc.Bacc("TRN2", target_bir_lowering=False, num_devices=1)
    arrays = {f"in_{k}": v for k, v in lay_out(inputs, np).items()}
    t = {k[3:]: nc.dram_tensor(k, v.shape, mybir.dt.from_np(v.dtype), kind="ExternalInput").ap()
         for k, v in arrays.items()}
    out = nc.dram_tensor("out", (1, S, D), F32, kind="ExternalOutput").ap()
    layer_kernel(nc, t, out)
    r = run_bass_kernel_spmd(nc, [arrays], core_ids=[0])
    return r.results[0]["out"]
```

```python
import math
from contextlib import ExitStack

import concourse.bass as bass
from concourse import mybir

F32 = mybir.dt.float32
BF16 = mybir.dt.bfloat16
I32 = mybir.dt.int32
U32 = mybir.dt.uint32
U8 = mybir.dt.uint8
ALU = mybir.AluOpType
ACT = mybir.ActivationFunctionType
AX = mybir.AxisListType

D = 1024
S = 1024
P = 128
NT = S // P
KT = D // P
RW_W, LRU_W, SBA_W = 384, 256, 384
HD = 64
C = 64
NPAIR = RW_W // P
RW_T, LRU_T, SBA_T = 11, 4, 6
RW_END = LRU_T + RW_T
CT = RW_T + LRU_T + SBA_T
V_COL = CT * P
IN_COLS = V_COL + SBA_W
HB = 512
E_N, E_G, G_E, E_F = 16, 4, 4, 512
FT = E_F // P
ALPHA = 2.0 ** 0.25
DECAY = math.exp(-0.5)
NQ = NT // 2
NB = NPAIR * NQ
LEVELS = 6
NEG = -1e30
ROWS = 2 * S + P
MAXB = 2 * S // P + E_N


def wait(e, sem, v):
    if v > 0:
        e.wait_ge(sem, v)


def layer_kernel(nc, t, out, stop=None):
    ctx = ExitStack()
    with ctx:
        def sb(name, shape, dt=F32):
            return ctx.enter_context(nc.sbuf_tensor(name, shape, dt))

        def sem(name):
            return ctx.enter_context(nc.semaphore(name))

        ident = sb("ident", [P, P])
        identb = sb("identb", [P, P], BF16)
        causal_neg = sb("causal_neg", [P, P], BF16)
        head_ones = sb("head_ones", [P, P])
        mask4 = sb("mask4", [P, 4, P], BF16)
        ident2 = sb("ident2", [P, C])
        lower = sb("lower", [P, LEVELS, P], U8)
        upper = sb("upper", [P, LEVELS, P], U8)
        restart = sb("restart", [P, S], BF16)
        vec = sb("vec", [P, 96])
        consts = sb("consts", [P, 8])
        w_up = sb("w_up", [P, RW_W])
        g_up = sb("g_up", [P, RW_W])
        lru_w = sb("lru_w", [P, 2, 2, HD])
        pc = sb("pc", [P, NPAIR, S // C])

        RW = sb("RW", [P, RW_T, S])
        KB = sb("KB", [P, 6, S])
        YT = sb("YT", [P, KT, S])
        SQ = sb("SQ", [P, 9, S])
        XS = sb("XS", [P, 12, S])
        TT = sb("TT", [P, 3, S])
        SV = SQ[:, 6:9, :].rearrange("p a b -> p (a b)").rearrange("p (n c) -> p n c", c=SBA_W)

        nvec = [0]

        def vcol(n):
            a = nvec[0]
            nvec[0] += n
            return a
        V_MU = vcol(RW_T)
        V_W0, V_A0, V_KK, V_KA, V_RK, V_LNG, V_LNB, V_SG = [vcol(3) for _ in range(8)]
        V_CW, V_CB, V_BA, V_BX, V_LAM, V_LG = vcol(8), vcol(2), vcol(2), vcol(2), vcol(2), vcol(2)
        V_LAST = nvec[0]
        V_NMU, V_NKA = vcol(RW_T), vcol(3)
        V_C, V_NC, V_L1, V_L2 = vcol(2), vcol(2), vcol(2), vcol(2)
        assert nvec[0] <= 96

        def v1(i):
            return vec[:, i:i + 1]

        PS = [ctx.enter_context(nc.psum_tensor(f"PS{i}", [P, 2 * HB], F32)) for i in range(4)]

        s_const = sem("consts_loaded")
        s_derived = sem("derived_consts_dve")
        s_lamc = sem("lambda_steps_act")
        s_masks = sem("masks_built_pool")
        s_masksd = sem("masks_built_dve")
        s_x = [sem(f"x_loaded{i}") for i in range(NT)]
        s_w = [sem(f"w_in_loaded{i}") for i in range(4)]
        s_pp = sem("proj_in_psum")
        s_pa = sem("shift_kept_by_act")
        s_pd = sem("shift_done_by_dve")
        s_pe = sem("proj_copied_by_act")
        s_ld, s_la, s_lp = sem("lru_dve"), sem("lru_act"), sem("lru_pe")
        s_rd, s_ra, s_rp = sem("rwkv_dve"), sem("rwkv_act"), sem("rwkv_pe")
        s_md, s_ma, s_mp, s_mo = sem("delta_dve"), sem("delta_act"), sem("delta_pe"), sem("delta_pool")
        s_wo, s_rc, s_op = sem("w_out_loaded"), sem("router_consts_loaded"), sem("mixed_in_psum")
        s_xr = [sem(f"x_rows_loaded{i}") for i in range(4)]
        s_n1d, s_n1a = sem("norm1_dve"), sem("norm1_act")
        s_x1p, s_x1t, s_lg = sem("x1_transposed"), sem("x1T_copied"), sem("logits_in_psum")
        s_rpool, s_q, s_qd, s_qa, s_qp = [sem(f"router_{x}") for x in ("pool", "chain", "dve", "act", "pe")]
        s_slot, s_tab, s_row = sem("slots_ready"), sem("block_table_ready"), sem("block_rows_ready")
        s_hot, s_idp, s_idx, s_x1d = [sem(x) for x in ("dispatch_one_hots", "tokens_in_psum", "block_tokens", "x1_stored")]
        s_pick = sem("block_tokens_picked")
        s_wg, s_wu, s_wd = [[sem(f"{x}_loaded{k}") for k in range(2)] for x in ("w_gate", "w_up", "w_down")]
        s_xg, s_xgp, s_ta, s_td = sem("block_rows"), sem("block_transposed"), sem("xgT_act"), sem("xgT_dve")
        s_g1, s_u1, s_si, s_hd = sem("gate_in_psum"), sem("up_in_psum"), sem("silu_done"), sem("hidden_done")
        s_htp, s_htd, s_y1 = sem("hidden_transposed"), sem("hiddenT_copied"), sem("down_in_psum")
        s_hd2, s_htp2, s_hta = sem("hidden_done_2"), sem("hidden_transposed_2"), sem("hiddenT_copied_2_act")
        s_ya, s_yd, s_ys = sem("y_act"), sem("y_dve"), sem("y_stored")
        s_gt = [sem(f"y_gathered{i}") for i in range(2 * NT)]
        s_tick = [sem("sp_passed_wait"), sem("pool_passed_wait")]
        s_l2, s_n2a, s_out, s_scaled = sem("norm2_consts"), sem("norm2_act"), sem("out_stored"), sem("x1_scaled")
        s_f1, s_f2, s_f3, s_f4 = [sem(f"norm2_{x}") for x in ("sums", "bias", "times_gain", "plus_bias")]
        s_init = sem("identities_set")
        s_tl, s_ul = sem("inverse_level"), sem("inverse_transposed_level")
        s_bz, s_bx, s_bv = sem("z_in_psum"), sem("attn_transposed"), sem("attn_v_in_psum")
        s_bd, s_ba, s_bt, s_bo = sem("attn_dve"), sem("attn_act"), sem("attnT_copied"), sem("attn_out_copied")
        s_ns = sem("head_squares_act")
        s_na, s_np, s_nd = sem("head_norm_act"), sem("head_norm_pe"), sem("head_norm_dve")
        s_fd, s_fa, s_fp = sem("rwkv_norm_dve"), sem("rwkv_norm_act"), sem("rwkv_norm_pe")

        const_loads = [(vec[:, 0:V_LAST], t["vecs"]), (w_up[:, :], t["lora_up"]), (g_up[:, :], t["g_up"]),
                       (lru_w[:, :, :, :], t["lru_w"])]
        CONSTS = 16 * len(const_loads)

        block = ctx.enter_context(nc.Block())

        def proj_sp(e):
            for ct in range(CT):
                if ct >= 4:
                    wait(e, s_pp, ct - 3)
                e.dma_start(XS[:, 8 + ct % 4, :], t["w_in"][ct]).then_inc(s_w[ct % 4], 16)
                if ct == 0:
                    for kt in range(KT):
                        e.dma_start(XS[:, kt, :], t["xT"][kt]).then_inc(s_x[kt], 16)
            wait(e, s_pp, CT - 1)
            e.dma_start(XS[:, 9:12, :].rearrange("p a b -> p (a b)"), t["w_v"]).then_inc(s_w[1], 16)

        def proj_free(e, n):
            if n >= 2:
                m = n - 2
                if LRU_T <= m < RW_END:
                    wait(e, s_pd, m - LRU_T + 1)
                else:
                    wait(e, s_pe, m + 1 if m < LRU_T else m - RW_T + 1)

        def proj_pe(e, n):
            proj_free(e, n)
            acc = PS[n % 2]
            if n < CT:
                wait(e, s_w[n % 4], 16 * (n // 4 + 1))
                for half in range(2):
                    for kt in range(KT):
                        if n == 0 and half == 0:
                            wait(e, s_x[kt], 16)
                        m = e.matmul(acc[:, half * HB:(half + 1) * HB], XS[:, 8 + n % 4, kt * P:(kt + 1) * P],
                                     XS[:, kt, half * HB:(half + 1) * HB], start=kt == 0, stop=kt == KT - 1)
            else:
                i = n - CT
                if i == 0:
                    wait(e, s_w[1], 16 * 6)
                wv = XS[:, 9:12, :].rearrange("p a b -> p (a b)").rearrange("p (k c) -> p k c", k=KT)
                for kt in range(KT):
                    m = e.matmul(acc[:, 0:SBA_W], XS[:, kt, i * P:(i + 1) * P], wv[:, kt, :],
                                 start=kt == 0, stop=kt == KT - 1)
            m.then_inc(s_pp, 1)

        def proj_act(e, n):
            wait(e, s_pp, n + 1)
            if n < LRU_T:
                e.copy(YT[:, 3 + n, :], PS[n % 2][:, :]).then_inc(s_pe, 1)
            elif n < RW_END:
                r = n - LRU_T
                wait(e, s_derived, 1)
                e.activation(RW[:, r, :], PS[n % 2][:, :], ACT.Identity, scale=v1(V_NMU + r)).then_inc(s_pa, 1)
            elif n < RW_END + NPAIR:
                e.mul(SQ[:, n - RW_END, :], PS[n % 2][:, :], HD ** -0.5).then_inc(s_pe, 1)
            elif n < CT:
                e.copy(SQ[:, n - RW_END, :], PS[n % 2][:, :]).then_inc(s_pe, 1)
            else:
                e.copy(SV[:, n - CT, :], PS[n % 2][:, 0:SBA_W]).then_inc(s_pe, 1)

        def proj_dve(e, r):
            wait(e, s_pa, r + 1)
            e.scalar_tensor_tensor(RW[:, r, 1:S], PS[(r + LRU_T) % 2][:, 0:S - 1], v1(V_MU + r), RW[:, r, 1:S],
                                   ALU.mult, ALU.add).then_inc(s_pd, 1)

        LD, LA, LP = 14, 12, 3

        def exp_ln(e):
            e.preload_act_table_set("natural_log_exp_and_others")

        def lru_bufs(u):
            return KB[:, 3 * u, :], KB[:, 3 * u + 1, :], KB[:, 3 * u + 2, :], TT[:, u, :], YT[:, 3 + u, :], YT[:, 5 + u, :]

        def lru_dve(e, u):
            A, B, Cc, Dd, G, X = lru_bufs(u)
            n = [u * LD]

            def step(ins):
                ins.then_inc(s_ld, 1)
                n[0] += 1
                return n[0]

            def own():
                wait(e, s_ld, n[0])
            wait(e, s_pe, LRU_T)
            own()
            step(e.tensor_scalar(A, X, v1(V_CW + 2 * 3 + u), v1(V_CB + u), ALU.mult, ALU.add))
            for back in range(1, 4):
                own()
                step(e.scalar_tensor_tensor(A[:, back:S], X[:, 0:S - back], v1(V_CW + 2 * (3 - back) + u),
                                            A[:, back:S], ALU.mult, ALU.add))
            yield
            wait(e, s_la, u * LA + 1)
            own()
            step(e.tensor_scalar(B, B, 0.044715, 1.0, ALU.mult, ALU.add))
            own()
            step(e.tensor_tensor(B, B, G, ALU.mult))
            wait(e, s_la, u * LA + 2)
            own()
            step(e.scalar_tensor_tensor(G, B, 1.0, G, ALU.add, ALU.mult))
            wait(e, s_la, u * LA + 4)
            own()
            step(e.tensor_tensor(Dd, Dd, A, ALU.mult))
            yield
            wait(e, s_la, u * LA + 5)
            own()
            step(e.tensor_scalar_max(B, B, 2.0 ** -62))
            wait(e, s_la, u * LA + 8)
            own()
            step(e.tensor_tensor(A, X, A, ALU.subtract))
            wait(e, s_la, u * LA + 9)
            own()
            step(e.tensor_tensor(Dd, Dd, A, ALU.mult))
            own()
            step(e.tensor_tensor_scan(A, Cc, Dd, 0.0, ALU.mult, ALU.add))
            own()
            step(e.scalar_tensor_tensor(A, G, 0.5, A, ALU.mult, ALU.mult))
            yield
            wait(e, s_la, u * LA + 12)
            own()
            step(e.scalar_tensor_tensor(G, A, v1(V_LG + u), B, ALU.mult, ALU.mult))

        def lru_act(e, u, part):
            A, B, Cc, Dd, G, X = lru_bufs(u)
            if part == 0:
                wait(e, s_pe, LRU_T)
                wait(e, s_la, u * LA + 0)
                e.activation(B, G, ACT.Square).then_inc(s_la, 1)
                wait(e, s_ld, u * LD + 6)
                wait(e, s_la, u * LA + 1)
                e.activation(B, B, ACT.Tanh, scale=0.7978845608028654).then_inc(s_la, 1)
                wait(e, s_lp, u * LP + 1)
                wait(e, s_la, u * LA + 2)
                e.activation(Cc, PS[2][:, :], ACT.Sigmoid, bias=v1(V_BA + u)).then_inc(s_la, 1)
                wait(e, s_lp, u * LP + 2)
                wait(e, s_la, u * LA + 3)
                e.activation(Dd, PS[3][:, :], ACT.Sigmoid, bias=v1(V_BX + u)).then_inc(s_la, 1)
                wait(e, s_ld, u * LD + 7)
                wait(e, s_masksd, 1)
                wait(e, s_la, u * LA + 4)
                e.activation(B, Cc, ACT.Tanh, scale=v1(V_C + u)).then_inc(s_la, 1)
                return
            if part == 2:
                wait(e, s_lp, u * LP + 3)
                wait(e, s_la, u * LA + 10)
                e.activation(B, PS[2][:, :], ACT.Ln, scale=1.0 / HD, bias=consts[:, 0:1]).then_inc(s_la, 1)
                wait(e, s_la, u * LA + 11)
                e.activation(B, B, ACT.Exp, scale=-0.5).then_inc(s_la, 1)
                return
            exp_ln(e)
            wait(e, s_la, u * LA + 5)
            e.activation(Cc, Cc, ACT.Exp, scale=v1(V_NC + u)).then_inc(s_la, 1)
            wait(e, s_ld, u * LD + 9)
            wait(e, s_la, u * LA + 6)
            e.activation(A, B, ACT.Ln, bias=1.0).then_inc(s_la, 1)
            wait(e, s_la, u * LA + 7)
            e.activation(X, B, ACT.Ln, scale=2.0).then_inc(s_la, 1)
            wait(e, s_ld, u * LD + 10)
            wait(e, s_la, u * LA + 8)
            e.activation(A, A, ACT.Exp, scale=0.5).then_inc(s_la, 1)
            wait(e, s_ld, u * LD + 13)
            wait(e, s_la, u * LA + 9)
            e.activation(B, A, ACT.Square).then_inc(s_la, 1)

        def heads_sum(e, acc, src):
            for half in range(2):
                m = e.matmul(acc[:, half * HB:(half + 1) * HB], head_ones[:, :], src[:, half * HB:(half + 1) * HB],
                             start=True, stop=True)
            return m

        def lru_pe(e, u, part):
            A, B = lru_bufs(u)[0:2]
            if part < 2:
                if part == 0:
                    wait(e, s_masksd, 1)
                    wait(e, s_const, CONSTS)
                    wait(e, s_ld, u * LD + 4)
                    wait(e, s_la, (u - 1) * LA + 11 if u else 0)
                for half in range(2):
                    for b in range(2):
                        q = slice(b * HD, (b + 1) * HD)
                        m = e.matmul(PS[2 + part][q, half * HB:(half + 1) * HB], lru_w[q, part, u, :],
                                     A[q, half * HB:(half + 1) * HB], start=True, stop=True)
                m.then_inc(s_lp, 1)
                return
            wait(e, s_la, u * LA + 10)
            heads_sum(e, PS[2], B).then_inc(s_lp, 1)

        RD, RA, RP = 14, 8, 4

        def rw_bufs(g):
            T = [TT[:, i, :] for i in range(3)] if g != 1 else [YT[:, 5 + i, :] for i in range(3)]
            return T + [KB[:, g, :], KB[:, 3 + g, :], YT[:, g, :], RW[:, g, :], RW[:, 3 + g, :], RW[:, 6 + g, :]]

        def rw_pre_act(e):
            wait(e, s_pd, RW_T)
            e.activation(RW[0:HD, 9, :], RW[0:HD, 9, :], ACT.Tanh)
            e.activation(RW[:, 10, :], RW[:, 10, :], ACT.Sigmoid).then_inc(s_ra, 1)

        def rw_act(e, g, part):
            T1, T2, T3, K, B, Y, r, k, v = rw_bufs(g)
            a0, d0, p0 = g * RA + 1, g * RD, g * RP
            if part == 0:
                if g == 0:
                    wait(e, s_ld, 2 * LD)
                if g == 2:
                    wait(e, s_rd, RD)
                wait(e, s_rp, p0 + 1)
                wait(e, s_ra, a0 + 0)
                e.activation(T1, PS[2][:, :], ACT.Sigmoid, bias=v1(V_W0 + g)).then_inc(s_ra, 1)
                wait(e, s_rp, p0 + 2)
                wait(e, s_ra, a0 + 1)
                e.activation(T3, PS[3][:, :], ACT.Sigmoid, bias=v1(V_A0 + g)).then_inc(s_ra, 1)
                wait(e, s_ra, a0 + 2)
                e.activation(Y, k, ACT.Square, scale=v1(V_KK + g)).then_inc(s_ra, 1)
                return
            exp_ln(e)
            wait(e, s_rd, d0 + 1)
            wait(e, s_ra, a0 + 3)
            e.activation(Y, Y, ACT.Ln, scale=2.0 ** 16).then_inc(s_ra, 1)
            wait(e, s_ra, a0 + 4)
            e.activation(Y, Y, ACT.Exp, scale=-0.5, bias=consts[:, 1:2]).then_inc(s_ra, 1)
            wait(e, s_rd, d0 + 3)
            wait(e, s_ra, a0 + 5)
            e.activation(T1, T1, ACT.Exp, scale=-DECAY).then_inc(s_ra, 1)
            wait(e, s_rd, d0 + 7)
            wait(e, s_ra, a0 + 6)
            e.activation(T3, T2, ACT.Exp, scale=-DECAY).then_inc(s_ra, 1)
            wait(e, s_ra, a0 + 7)
            e.activation(T2, T2, ACT.Exp, scale=DECAY).then_inc(s_ra, 1)

        def rw_dve(e, g):
            T1, T2, T3, K, B, Y, r, k, v = rw_bufs(g)
            a0, d0, p0 = g * RA + 1, g * RD, g * RP
            n = [d0]

            def step(ins):
                ins.then_inc(s_rd, 1)
                n[0] += 1

            def own():
                wait(e, s_rd, n[0])
            wait(e, s_ra, a0 + 3)
            wait(e, s_rp, p0 + 3)
            own()
            step(e.tensor_scalar_max(Y, PS[2][:, :], 1e-24))
            own()
            step(e.tensor_tensor_scan(T2, restart[:, :], T1, 0.0, ALU.mult, ALU.add))
            own()
            step(e.tensor_tensor(T1, T2, T1, ALU.subtract))
            wait(e, s_ra, a0 + 5)
            own()
            step(e.scalar_tensor_tensor(K, k, v1(V_KK + g), Y, ALU.mult, ALU.mult))
            own()
            step(e.tensor_tensor(B, K, T3, ALU.mult))
            own()
            step(e.tensor_scalar(T3, T3, v1(V_KA + g), v1(V_NKA + g), ALU.mult, ALU.add))
            own()
            step(e.tensor_tensor(k, k, T3, ALU.mult))
            own()
            step(e.scalar_tensor_tensor(Y, r, v1(V_RK + g), k, ALU.mult, ALU.mult))
            wait(e, s_ra, a0 + 6)
            own()
            step(e.tensor_tensor(K, K, T1, ALU.mult))
            wait(e, s_rp, p0 + 4)
            own()
            step(e.tensor_tensor(Y, PS[3][:, :], v, ALU.mult))
            wait(e, s_ra, a0 + 7)
            own()
            step(e.tensor_tensor(r, r, T3, ALU.mult))
            own()
            step(e.tensor_copy(pc[:, g, :], T3[:, C - 1:S:C]))
            wait(e, s_ra, a0 + 8)
            own()
            step(e.tensor_tensor(B, B, T2, ALU.mult))
            own()
            step(e.tensor_tensor(k, k, T2, ALU.mult))

        def rw_pe(e, g, part):
            T1, T2, T3, K, B, Y, r, k, v = rw_bufs(g)
            a0, d0 = g * RA + 1, g * RD
            if part == 0:
                wait(e, s_ra, 1)
                if g == 0:
                    wait(e, s_la, 2 * LA)
                else:
                    wait(e, s_rd, d0 - RD + 10)
                for rows, acc in ((slice(0, HD), PS[2]), (slice(HD, P), PS[3])):
                    for half in range(2):
                        m = e.matmul(acc[:, half * HB:(half + 1) * HB], w_up[rows, g * P:(g + 1) * P],
                                     RW[rows, 9, half * HB:(half + 1) * HB], start=True, stop=True)
                    m.then_inc(s_rp, 1)
            elif part == 1:
                wait(e, s_ra, a0 + 3)
                heads_sum(e, PS[2], Y).then_inc(s_rp, 1)
            else:
                wait(e, s_rd, d0 + 8)
                heads_sum(e, PS[3], Y).then_inc(s_rp, 1)


        s_iota = sem("iotas_by_pool")
        ip = TT[:, 0, 0:P].bitcast(I32)
        jf = TT[:, 0, P:2 * P].bitcast(I32)
        xr = TT[:, 0, 2 * P:3 * P].bitcast(I32)
        xrf, dff, m1, m2 = [TT[:, 0, (3 + i) * P:(4 + i) * P] for i in range(4)]

        def masks_pool(e):
            e.memset(ident[:, :], 0.0)
            e.memset(causal_neg[:, :], 0.0)
            e.iota(ip, [[0, P]], base=0, channel_multiplier=1)
            e.iota(jf, [[1, P]], base=0, channel_multiplier=0).then_inc(s_iota, 1)
            e.wait_ge(s_iota, 1)
            e.affine_select(out=ident[:, :], in_=ident[:, :], compare_op=ALU.not_equal, fill=1.0, base=0,
                            pattern=[[-1, P]], channel_multiplier=1)
            e.affine_select(out=causal_neg[:, :], in_=causal_neg[:, :], compare_op=ALU.is_gt, fill=NEG, base=0,
                            pattern=[[-1, P]], channel_multiplier=1).then_inc(s_masks, 1)
            for dst, src in const_loads:
                e.dma_start(dst, src).then_inc(s_const, 16)

        def masks_dve(e):
            n = [0]
            s_own = sem("mask_steps_dve")

            def step(ins):
                ins.then_inc(s_own, 1)
                n[0] += 1
                e.wait_ge(s_own, n[0])
            step(e.memset(restart[:, :], 1.0))
            for i, x in enumerate((1e-6, 8 * math.log(2.0), 64e-5, 1e-5)):
                ins = e.memset(consts[:, i:i + 1], x)
            step(ins)
            step(e.memset(restart[:, 0:S:C], 0.0))
            wait(e, s_masks, 1)
            step(e.tensor_copy(identb[:, :], ident[:, :]))
            step(e.tensor_tensor(xr, ip, jf, ALU.bitwise_xor))
            step(e.tensor_copy(xrf, xr))
            step(e.tensor_tensor(dff, jf, ip, ALU.subtract))
            step(e.tensor_single_scalar(head_ones[:, :], xr, C, ALU.is_lt))
            step(e.tensor_tensor(ident2[:, :], ident[:, 0:C], ident[:, C:P], ALU.add))
            step(e.tensor_single_scalar(m1, dff, 0.0, ALU.is_gt))
            step(e.tensor_single_scalar(m2, dff, 0.0, ALU.is_ge))
            step(e.scalar_tensor_tensor(mask4[:, 0, :], m1, -1.0, head_ones[:, :], ALU.mult, ALU.mult))
            step(e.tensor_tensor(mask4[:, 1, :], m2, head_ones[:, :], ALU.mult))
            step(e.tensor_tensor(mask4[:, 2, :], m1, head_ones[:, :], ALU.mult))
            step(e.tensor_tensor(mask4[:, 3, :], m2, head_ones[:, :], ALU.mult))
            step(e.tensor_single_scalar(m2, dff, 0.0, ALU.is_lt))
            for lv in range(LEVELS):
                step(e.tensor_single_scalar(dff, xrf, float(1 << lv), ALU.is_ge))
                step(e.scalar_tensor_tensor(dff, xrf, float(2 << lv), dff, ALU.is_lt, ALU.mult))
                step(e.tensor_tensor(upper[:, lv, :], dff, m1, ALU.mult))
                step(e.tensor_tensor(lower[:, lv, :], dff, m2, ALU.mult))
            wait(e, s_const, CONSTS)
            e.tensor_scalar(vec[:, V_NMU:V_NMU + RW_T], vec[:, V_MU:V_MU + RW_T], -1.0, 1.0, ALU.mult, ALU.add)\
                .then_inc(s_derived, 1)
            step(e.tensor_scalar(vec[:, V_NKA:V_NKA + 3], vec[:, V_KA:V_KA + 3], -1.0, 1.0, ALU.mult, ALU.add))
            step(e.tensor_scalar(vec[:, V_C:V_C + 2], vec[:, V_LAM:V_LAM + 2], -1.0, 0.0, ALU.mult, ALU.max))
            e.wait_ge(s_lamc, 3)
            step(e.tensor_tensor(vec[:, V_C:V_C + 2], vec[:, V_C:V_C + 2], vec[:, V_L1:V_L1 + 2], ALU.add))
            step(e.tensor_scalar_mul(vec[:, V_NC:V_NC + 2], vec[:, V_C:V_C + 2], -8.0))
            step(e.tensor_scalar_mul(vec[:, V_C:V_C + 2], vec[:, V_C:V_C + 2], 8.0))
            e.tensor_copy(vec[:, V_L2:V_L2 + 2], vec[:, V_C:V_C + 2]).then_inc(s_masksd, 1)

        def lam_act(e):
            a = vec[:, V_L1:V_L1 + 2]
            wait(e, s_const, CONSTS)
            e.activation(a, vec[:, V_LAM:V_LAM + 2], ACT.Abs).then_inc(s_lamc, 1)
            e.wait_ge(s_lamc, 1)
            e.activation(a, a, ACT.Exp, scale=-1.0).then_inc(s_lamc, 1)
            e.wait_ge(s_lamc, 2)
            e.activation(a, a, ACT.Ln, bias=1.0).then_inc(s_lamc, 1)


        MP, MD, MA = 30, 10, 10
        NTL, NUL = LEVELS - 1, LEVELS

        def p_level(lv, what):
            return 8 + 3 * (lv - 1) + 1 + (what if lv < LEVELS - 1 else min(what, 1))
        P_T, P_HF, P_JG, P_ST = 23, 24, 25, 25
        XF = XS[:, :, :].rearrange("p a b -> p (a b)")
        off = [0]

        def lay(n):
            a = off[0]
            off[0] += n
            return XF[:, a:a + n]
        AM = lay(4 * 4 * P).rearrange("p (m k c) -> p m k c", m=4, k=4)
        T_ = lay(4 * P).rearrange("p (m c) -> p m c", m=4)
        U_ = lay(4 * P).rearrange("p (m c) -> p m c", m=4)
        M1 = lay(4 * P).rearrange("p (m c) -> p m c", m=4)
        RHS = lay(4 * P).rearrange("p (m c) -> p m c", m=4)
        WY = lay(4 * P).rearrange("p (m c) -> p m c", m=4)
        TOK = lay(2 * 3 * P).rearrange("p (i k c) -> p i k c", i=2, k=3)
        BKC = lay(2 * 2 * P).rearrange("p (k c) -> p k c", k=2)
        HF = lay(4 * P)
        JG = lay(4 * P)
        ST = lay(5 * C).rearrange("p (k c) -> p k c", k=5)
        Eb = [lay(S) for _ in range(2)]
        ATb = [lay(S) for _ in range(2)]
        assert off[0] <= 12 * S

        def RB(j):
            return PS[2 + j // 2][:, (j % 2) * HB:(j % 2 + 1) * HB]

        def four(x):
            return x.rearrange("p (m c) -> p m c", m=4)

        def mats_of(b):
            g, q = b // NQ, b % NQ
            return g, q, [(m, m // 2, slice((m % 2) * HD, (m % 2 + 1) * HD)) for m in range(4)]

        def mats_pool(e):
            for b in range(NB):
                g, q, _ = mats_of(b)
                wait(e, s_rd, RD * NPAIR)
                if b == 0:
                    wait(e, s_pp, CT + NT)
                wait(e, s_mp, (b - 1) * MP + 6 if b else 0)
                dec = pc[:, g, 4 * q:4 * q + 4].rearrange("p (n o) -> p n o", o=1).broadcast_to([P, 4, C])
                for k, src in enumerate((KB[:, 3 + g, :], RW[:, 3 + g, :])):
                    ins = e.tensor_tensor(BKC[:, k, :].rearrange("p (n c) -> p n c", c=C),
                                          src[:, 256 * q:256 * q + 256].rearrange("p (n c) -> p n c", c=C), dec,
                                          ALU.mult)
                ins.then_inc(s_mo, 1)
                wait(e, s_mp, (b - 1) * MP + P_T if b else 0)
                eye = ident[:, :].rearrange("p (o c) -> p o c", o=1).broadcast_to([P, 4, P])
                e.tensor_copy(T_[:, :, :], eye)
                e.tensor_copy(U_[:, :, :], eye).then_inc(s_init, 1)

        def keep_clock(e, bank, n):
            for _ in range(n):
                e.matmul(bank, identb[:, :], restart[:, 0:bank.shape[1]], start=True, stop=True)

        def mats_pe(e, b):
            g, q, ms = mats_of(b)
            P0, D0, A0 = b * MP, b * MD, b * MA
            Kq, Bt, Kt, Rt, V = KB[:, g, :], KB[:, 3 + g, :], RW[:, 3 + g, :], RW[:, g, :], RW[:, 6 + g, :]
            wait(e, s_rd, RD * NPAIR)
            wait(e, s_ra, RA * NPAIR + 1)
            wait(e, s_ma, A0)
            wait(e, s_fd, 4 * g)
            for m, i, h in ms:
                wait(e, s_md, D0 - (5, 1, 1, 0)[m] if b else 0)
                tk = slice((2 * q + i) * P, (2 * q + i + 1) * P)
                for k, (l, r) in enumerate(((Bt, Kq), (Bt, Rt), (Kt, Kq), (Kt, Rt))):
                    ins = e.matmul(RB(m)[:, k * P:(k + 1) * P], l[h, tk], r[h, tk], start=True, stop=True)
                ins.then_inc(s_mp, 1)
            wait(e, s_mo, b + 1)
            for i in range(2):
                wait(e, s_md, D0 + i + 1)
                tk = slice((2 * q + i) * P, (2 * q + i + 1) * P)
                for k, src in enumerate((Kq[:, tk], V[:, tk], BKC[:, 0, i * P:(i + 1) * P],
                                         BKC[:, 1, i * P:(i + 1) * P])):
                    ins = e.transpose(RB(i)[:, k * P:(k + 1) * P], src, ident[:, :])
                ins.then_inc(s_mp, 1)
            wait(e, s_md, D0 + 4)
            for m, i, h in ms:
                ins = e.transpose(RB(2)[:, m * P:(m + 1) * P], AM[:, m, 0, :], ident[:, :])
            ins.then_inc(s_mp, 1)
            yield
            wait(e, s_ma, A0 + 2)
            for m, i, h in ms:
                ins = e.matmul(RB(1)[:, m * HD:(m + 1) * HD], AM[:, m, 2, :], TOK[:, i, 0, h], start=True, stop=True)
            ins.then_inc(s_mp, 1)
            for lv in range(1, LEVELS):
                wait(e, s_tl, b * NTL + lv)
                for m, i, h in ms:
                    ins = e.matmul(RB(3)[:, m * P:(m + 1) * P], AM[:, m, 0, :], T_[:, m, :], start=True, stop=True)
                ins.then_inc(s_mp, 1)
                yield
                wait(e, s_ul, b * NUL + lv)
                wait(e, s_ma, A0 + 3 + lv)
                if lv < LEVELS - 1:
                    for m, i, h in ms:
                        ins = e.matmul(RB(2)[:, m * P:(m + 1) * P], U_[:, m, :], M1[:, m, :], start=True, stop=True)
                    ins.then_inc(s_mp, 1)
                for m, i, h in ms:
                    ins = e.matmul(RB(0)[:, m * P:(m + 1) * P], M1[:, m, :], U_[:, m, :], start=True, stop=True)
                ins.then_inc(s_mp, 1)
                yield
            wait(e, s_ul, (b + 1) * NUL)
            for m, i, h in ms:
                ins = e.matmul(RB(3)[:, m * P:(m + 1) * P], U_[:, m, :], RHS[:, m, :], start=True, stop=True)
            ins.then_inc(s_mp, 1)
            yield
            wait(e, s_ma, A0 + 9)
            for m, i, h in ms:
                e.matmul(RB(2)[h, i * P:(i + 1) * P], WY[:, m, 0:HD], AM[:, m, 1, :], start=True, stop=True)
            for m, i, h in ms:
                for c in range(2):
                    r = slice(c * C, (c + 1) * C)
                    ins = e.matmul(RB(2 - c)[h, 256 + i * C:256 + (i + 1) * C], WY[r, m, 0:HD],
                                   TOK[r, i, 1, h], start=True, stop=True)
            ins.then_inc(s_mp, 1)
            for m, i, h in ms:
                o = RB(0)[h, i * P:(i + 1) * P]
                e.matmul(o, WY[:, m, HD:P], AM[:, m, 1, :], start=True, stop=False)
                e.matmul(o, TOK[:, i, 0, h], AM[:, m, 3, :], start=False, stop=True)
            for m, i, h in ms:
                for c in range(2):
                    r = slice(c * C, (c + 1) * C)
                    o = RB(3 * c)[h, 256 + i * C:256 + (i + 1) * C]
                    e.matmul(o, TOK[r, i, 1, h], WY[r, m, HD:P], start=True, stop=False)
                    ins = e.matmul(o, TOK[r, i, 2, h], TOK[r, i, 0, h], start=False, stop=True)
            ins.then_inc(s_mp, 1)
            for c in range(4):
                yield
                if c == 1:
                    wait(e, s_ma, A0 + 10)
                if c >= 1:
                    keep_clock(e, RB(3)[:, 256:512], 4)
                wait(e, s_md, D0 + 5 + c)
                for hh in range(2):
                    h = slice(hh * HD, (hh + 1) * HD)
                    ins = e.matmul(RB(1)[h, c * C:(c + 1) * C], HF[h, 256 + c * C:256 + (c + 1) * C],
                                   ST[h, (4 * q + c) % 5, :], start=True, stop=True)
                ins.then_inc(s_mp, 1)
                if c == 0:
                    wait(e, s_ma, A0 + 10)
                for hh in range(2):
                    h = slice(hh * HD, (hh + 1) * HD)
                    ins = e.matmul(RB(3)[h, c * C:(c + 1) * C], ST[h, (4 * q + c) % 5, :],
                                   HF[h, c * C:(c + 1) * C], start=True, stop=True)
            ins.then_inc(s_mp, 1)

        def mats_act(e, b):
            g, q, ms = mats_of(b)
            P0, D0, A0 = b * MP, b * MD, b * MA
            for i in range(2):
                wait(e, s_mp, P0 + 5 + i)
                e.copy(RHS[:, 2 * i:2 * i + 2, 0:HD], RB(i)[:, 0:P].rearrange("p (h c) -> p h c", h=2))
                e.copy(TOK[:, i, :, :], RB(i)[:, P:4 * P].rearrange("p (k c) -> p k c", k=3)).then_inc(s_ma, 1)
            yield
            wait(e, s_mp, P0 + 8)
            e.copy(RHS[:, :, HD:P], RB(1)[:, 0:4 * HD].rearrange("p (m c) -> p m c", m=4)).then_inc(s_ma, 1)
            for lv in range(1, LEVELS):
                wait(e, s_mp, P0 + p_level(lv, 0))
                e.copy(M1[:, :, :], four(RB(3))).then_inc(s_ma, 1)
                yield
                yield
            wait(e, s_mp, P0 + P_T)
            e.mul(WY[:, :, :], four(RB(3)), -1.0).then_inc(s_ma, 1)
            yield
            wait(e, s_mp, P0 + P_JG)
            e.copy(JG[:, 0:256], RB(0)[:, 0:256])
            gc = JG[:, 256:512].rearrange("p (i c k) -> p i c k", i=2, c=2)
            for c in range(2):
                ins = e.copy(gc[:, :, c, :], RB(3 * c)[:, 256:384].rearrange("p (i k) -> p i k", i=2))
            ins.then_inc(s_ma, 1)
            for c in range(4):
                yield

        def mats_dve(e, b):
            g, q, ms = mats_of(b)
            P0, D0, A0 = b * MP, b * MD, b * MA

            def level(x, mask, lv, src):
                return e.copy_predicated(x[:, :, :], mask[:, lv:lv + 1, :].broadcast_to([P, 4, P]), src)
            for m in range(4):
                wait(e, s_mp, P0 + m + 1)
                e.tensor_tensor(AM[:, m, :, :], four(RB(m)), mask4[:, :, :], ALU.mult).then_inc(s_md, 1)
            wait(e, s_init, b + 1)
            wait(e, s_mp, P0 + 7)
            level(T_, lower, 0, four(RB(2))).then_inc(s_tl, 1)
            wait(e, s_md, D0 + 4)
            level(U_, upper, 0, AM[:, :, 0, :]).then_inc(s_ul, 1)
            yield
            for lv in range(1, LEVELS):
                yield
                if lv < LEVELS - 1:
                    wait(e, s_tl, b * NTL + lv)
                    wait(e, s_mp, P0 + p_level(lv, 1))
                    level(T_, lower, lv, four(RB(2))).then_inc(s_tl, 1)
                wait(e, s_ul, b * NUL + lv)
                wait(e, s_mp, P0 + p_level(lv, 2))
                level(U_, upper, lv, four(RB(0))).then_inc(s_ul, 1)
                yield
            yield
            wait(e, s_mp, P0 + P_HF)
            e.tensor_tensor(HF[:, 0:256], RB(2)[:, 0:256], RW[:, g, 256 * q:256 * q + 256], ALU.add)
            if q == 0:
                e.memset(ST[:, 0, :], 0.0)
            for c in range(4):
                ins = e.scalar_tensor_tensor(HF[:, 256 + c * C:256 + (c + 1) * C], ident2[:, :],
                                             pc[:, g, 4 * q + c:4 * q + c + 1],
                                             RB(2 - c % 2)[:, 256 + (c // 2) * C:256 + (c // 2 + 1) * C],
                                             ALU.mult, ALU.add)
            ins.then_inc(s_md, 1)
            yield
            wait(e, s_ma, A0 + 10)
            for c in range(4):
                wait(e, s_mp, P0 + P_ST + 1 + c)
                e.tensor_tensor(ST[:, (4 * q + c + 1) % 5, :], RB(1)[:, c * C:(c + 1) * C],
                                JG[:, 256 + c * C:256 + (c + 1) * C], ALU.add).then_inc(s_md, 1)
                if c < 3:
                    yield
            wait(e, s_mp, P0 + MP)
            e.tensor_tensor(KB[:, g, 256 * q:256 * q + 256], RB(3)[:, 0:256], JG[:, 0:256], ALU.add)\
                .then_inc(s_md, 1)

        def side_by_side(mats, piece, e, b):
            for k, _ in enumerate(mats(e, b)):
                if b + k:
                    piece(e, batch_step(b) + k)

        GAPS = 16

        def batch_step(b):
            return GAPS * b + 4 * (b // NQ) - 1

        def norm_step(g):
            return batch_step(NQ * (g + 1) - 1) + GAPS

        def snorms(g):
            return range(g - 1, g) if 0 < g < NPAIR - 1 else range(NPAIR - 2, NPAIR) if g else ()

        def rnorm_pe(e, g):
            O = KB[:, g, :]
            wait(e, s_md, (g + 1) * NQ * MD)
            heads_sum(e, PS[2], O).then_inc(s_fp, 1)
            for x in snorms(g):
                snorm_pe(e, x)
            j = norm_step(g)
            sba_pe(e, j)
            sba_pe(e, j + 1)
            wait(e, s_fd, 4 * g + 1)
            for half in range(2):
                ins = e.matmul(PS[2][:, half * HB:(half + 1) * HB], g_up[:, g * P:(g + 1) * P],
                               RW[:, 10, half * HB:(half + 1) * HB], start=True, stop=True)
            ins.then_inc(s_fp, 1)
            sba_pe(e, j + 2)
            wait(e, s_fa, 3 * g + 1)
            heads_sum(e, PS[3], TT[:, 1, :]).then_inc(s_fp, 1)
            sba_pe(e, j + 3)

        def rnorm_act(e, g):
            x = TT[:, 1, :]
            for xg in snorms(g):
                snorm_act(e, xg, 0)
            wait(e, s_fd, 4 * g + 1)
            e.activation(x, KB[:, g, :], ACT.Square).then_inc(s_fa, 1)
            for xg in snorms(g):
                snorm_act(e, xg, 1)
            for j in range(norm_step(g), norm_step(g) + 4):
                sba_act(e, j)
            wait(e, s_fp, 3 * g + 3)
            wait(e, s_fa, 3 * g + 1)
            e.activation(x, PS[3][:, :], ACT.Ln, scale=1.0 / HD, bias=consts[:, 2:3]).then_inc(s_fa, 1)
            wait(e, s_fa, 3 * g + 2)
            e.activation(x, x, ACT.Exp, scale=-0.5).then_inc(s_fa, 1)

        def rnorm_dve(e, g):
            O, Y = KB[:, g, :], YT[:, g, :]
            wait(e, s_md, (g + 1) * NQ * MD)
            wait(e, s_fp, 3 * g + 1)
            e.scalar_tensor_tensor(O, PS[2][:, :], -1.0 / HD, O, ALU.mult, ALU.add).then_inc(s_fd, 1)
            for x in snorms(g):
                snorm_dve(e, x)
            for j in range(norm_step(g), norm_step(g) + 3):
                sba_dve(e, j)
            wait(e, s_fd, 4 * g + 1)
            wait(e, s_fa, 3 * g + 3)
            e.scalar_tensor_tensor(O, O, v1(V_LNG + g), TT[:, 1, :], ALU.mult, ALU.mult).then_inc(s_fd, 1)
            wait(e, s_fd, 4 * g + 2)
            e.scalar_tensor_tensor(Y, O, v1(V_LNB + g), Y, ALU.add, ALU.add).then_inc(s_fd, 1)
            wait(e, s_fd, 4 * g + 3)
            wait(e, s_fp, 3 * g + 2)
            e.tensor_tensor(Y, Y, PS[2][:, :], ALU.mult).then_inc(s_fd, 1)
            sba_dve(e, norm_step(g) + 3)

        NU = NPAIR * NT * 2
        Rl = TT[:, 0, :]

        def unit(u):
            g, n, hh = u // (2 * NT), (u // 2) % NT, u % 2
            i = n // 2 if n % 2 == 0 else NT - 1 - n // 2
            return g, i, hh, slice(hh * HD, (hh + 1) * HD), (i + 1) * P, 1 + (i > 0)

        def group(i, k):
            cut = (i + 2) // 2
            return (0, cut) if k == 0 else (cut, i + 1)

        def groups(u):
            return sum(unit(x)[5] for x in range(u))
        BD, BA = 3, 4

        def sba_pe(e, j):
            u, kind = j // 4, j % 4
            if kind == 0:
                if u >= NU:
                    return
                g, i, hh, h, kv, ng = unit(u)
                wait(e, s_pe, LRU_T + SBA_T + NT)
                wait(e, s_bd, BD * u)
                for ng_ in range(1, NPAIR - 1):
                    if j == norm_step(ng_) + 1:
                        wait(e, s_na, 2 * (ng_ - 1) + 1)
                for lo in range(0, kv, HB):
                    hi = min(kv, lo + HB)
                    last = hi == kv
                    ins = e.matmul(PS[0][:, lo:hi], SQ[h, g, i * P:(i + 1) * P], SQ[h, 3 + g, lo:hi],
                                   start=True, stop=not last)
                ins = e.matmul(PS[0][:, kv - P:kv], identb[:, :], causal_neg[:, :], start=False, stop=True)
                ins.then_inc(s_bz, 1)
                return
            u -= 1
            if not 0 <= u < NU:
                return
            g, i, hh, h, kv, ng = unit(u)
            if kind <= ng:
                k = kind - 1
                wait(e, s_ba, BA * u + 4)
                wait(e, s_bt, groups(u) + k)
                lo, hi = group(i, k)
                for st in range(lo, hi):
                    ins = e.transpose(PS[1][:, (st - lo) * P:(st - lo + 1) * P], Eb[u % 2][:, st * P:(st + 1) * P],
                                      ident[:, :])
                ins.then_inc(s_bx, 1)
            if kind == 3:
                wait(e, s_bt, groups(u + 1))
                if hh == 0:
                    wait(e, s_bo, u // 2)
                for st in range(i + 1):
                    ins = e.matmul(PS[1][h, HB + (i % 4) * P:HB + (i % 4 + 1) * P],
                                   SV[:, st, g * P + hh * HD:g * P + (hh + 1) * HD],
                                   ATb[u % 2][:, st * P:(st + 1) * P], start=st == 0, stop=st == i)
                ins.then_inc(s_bv, 1)

        def sba_act(e, j):
            u, kind = j // 4, j % 4
            if kind == 0:
                if 1 <= u <= NU:
                    E_ = Eb[(u - 1) % 2][:, 0:unit(u - 1)[4]]
                    wait(e, s_bd, BD * u)
                    e.activation(E_, E_, ACT.Exp).then_inc(s_ba, 1)
                if 2 <= u < NU + 2 and u % 2 == 1:
                    g, i, hh, h, kv, ng = unit(u - 2)
                    wait(e, s_bv, u - 1)
                    e.copy(YT[:, 5 + g, i * P:(i + 1) * P], PS[1][:, HB + (i % 4) * P:HB + (i % 4 + 1) * P])\
                     .then_inc(s_bo, 1)
                if u >= NU:
                    return
                kv = unit(u)[4]
                E_ = Eb[u % 2][:, 0:kv]
                wait(e, s_bz, u + 1)
                if u == 0:
                    wait(e, s_pp, CT + NT)
                wait(e, s_bx, groups(u - 1) if u > 1 else 0)
                e.activation(E_, PS[0][:, 0:kv], ACT.Abs).then_inc(s_ba, 1)
                e.wait_ge(s_ba, BA * u + 1)
                e.activation(E_, E_, ACT.Exp, scale=-1.0).then_inc(s_ba, 1)
                e.wait_ge(s_ba, BA * u + 2)
                e.activation(E_, E_, ACT.Ln, bias=1.0).then_inc(s_ba, 1)

        def sba_scan(e, u):
            kv = unit(u)[4]
            E_, R_ = Eb[u % 2][:, 0:kv], Rl[:, 0:kv]
            wait(e, s_ba, BA * u + 3)
            wait(e, s_bd, BD * u + 1)
            e.tensor_tensor_scan(R_[:, ::-1], E_[:, ::-1], R_[:, ::-1], 0.0, ALU.add, ALU.add).then_inc(s_bd, 1)
            wait(e, s_bd, BD * u + 2)
            e.tensor_tensor(E_, PS[0][:, 0:kv], R_, ALU.subtract).then_inc(s_bd, 1)

        def sba_dve(e, j, scan=True):
            u, kind = j // 4, j % 4
            if kind in (1, 2) and 1 <= u <= NU and kind <= unit(u - 1)[5]:
                v, k = u - 1, kind - 1
                i = unit(v)[1]
                wait(e, s_bx, groups(v) + k + 1)
                wait(e, s_bv, v - 1)
                lo, hi = group(i, k)
                e.tensor_copy(ATb[v % 2][:, lo * P:hi * P], PS[1][:, 0:(hi - lo) * P]).then_inc(s_bt, 1)
            if u >= NU:
                return
            if kind == 1:
                kv = unit(u)[4]
                wait(e, s_bz, u + 1)
                wait(e, s_bd, BD * u)
                wait(e, s_ba, BA * u + 1)
                e.tensor_scalar_max(Rl[:, 0:kv], PS[0][:, 0:kv], 0.0).then_inc(s_bd, 1)
            if kind == 2 and scan:
                sba_scan(e, u)

        SN = [(TT[:, 2, :], PS[0]), (TT[:, 2, :], PS[0]), (TT[:, 0, :], PS[1])]

        def snorm_act(e, g, part):
            x, sums = SN[g]
            if part == 0:
                wait(e, s_bo, NT * (g + 1))
                wait(e, s_nd, min(g, 1))
                if g == NPAIR - 1:
                    wait(e, s_bd, BD * NU)
                e.activation(x, YT[:, 5 + g, :], ACT.Square).then_inc(s_ns, 1)
                return
            wait(e, s_np, g + 1)
            e.activation(x, sums[:, :], ACT.Ln, scale=1.0 / HD, bias=consts[:, 0:1]).then_inc(s_na, 1)
            wait(e, s_na, 2 * g + 1)
            e.activation(x, x, ACT.Exp, scale=-0.5).then_inc(s_na, 1)

        def snorm_pe(e, g):
            x, sums = SN[g]
            wait(e, s_ns, g + 1)
            wait(e, s_bd, BD * min((norm_step(g + 1) + 1) // 4, NU))
            heads_sum(e, sums, x).then_inc(s_np, 1)

        def snorm_dve(e, g):
            wait(e, s_na, 2 * g + 2)
            e.scalar_tensor_tensor(YT[:, 5 + g, :], YT[:, 5 + g, :], v1(V_SG + g), SN[g][0], ALU.mult, ALU.mult)\
                .then_inc(s_nd, 1)

        WO = [RW[:, 0, :], RW[:, 3, :], RW[:, 6, :], RW[:, 1, :], RW[:, 4, :], RW[:, 7, :], KB[:, 3, :], KB[:, 4, :]]
        XR = [KB[:, 0, :], KB[:, 1, :], KB[:, 2, :], KB[:, 5, :]]
        LN1 = [RW[:, 2, :], RW[:, 5, :]]
        LN2 = [TT[:, 1, :], TT[:, 2, :]]
        X1 = SQ[:, 0:NT, :]
        X1T = TT[:, 0, :]
        RX = RW[:, 8:11, :].rearrange("p a b -> p (a b)")
        roff = [0]

        def small(n):
            a = roff[0]
            roff[0] += n
            return RX[:, a:a + n]
        before, ones = small(P), small(P)
        rt_w = small(KT * E_N)
        rt_b = small(E_N)
        stats, mv = small(2 * 12).rearrange("p (b c) -> p b c", b=2), small(2 * 4).rearrange("p (b c) -> p b c", b=2)
        slot = small(2 * NT).bitcast(U32).rearrange("p (k i) -> p k i", k=2)
        gate = small(2 * NT).rearrange("p (k i) -> p k i", k=2)
        tab = small(64).bitcast(I32)
        blk_iota = small((MAXB + 1) * E_N)
        NCOL = MAXB + 1
        col_iota, row_iota, token = small(NCOL).bitcast(I32), small(P).bitcast(I32), small(NT)
        block_tok = small(NCOL).bitcast(U32)
        cur_tok = small(1).bitcast(U32)
        rev4, rev16 = small(G_E), small(E_N)
        NORM_D, NORM_A = 6, 3

        def norm_dve(e, i, sd, sa, x, res, g, b, d0, a0):
            st, m = stats[:, i % 2, :], mv[:, i % 2, :]
            for half in range(2):
                ins = e.bn_stats(st[:, 6 * half:6 * half + 6], x[:, half * HB:(half + 1) * HB])
            ins.then_inc(sd, 1)
            wait(e, sd, d0 + 1)
            e.bn_aggr(m[:, 0:2], st).then_inc(sd, 1)
            wait(e, sd, d0 + 2)
            wait(e, sa, a0 + 2)
            e.scalar_tensor_tensor(m[:, 3:4], m[:, 0:1], -1.0, m[:, 2:3], ALU.mult, ALU.mult).then_inc(sd, 1)
            wait(e, sa, a0 + 3)
            e.tensor_tensor(x, x, g, ALU.mult).then_inc(sd, 1)
            wait(e, sd, d0 + 4)
            e.tensor_tensor(res, x, b, ALU.add).then_inc(sd, 1)

        def norm_act(e, i, sd, sa, x, d0, a0):
            m = mv[:, i % 2, :]
            wait(e, sa, a0)
            wait(e, sd, d0 + 2)
            e.activation(m[:, 2:3], m[:, 1:2], ACT.Ln, bias=consts[:, 3:4]).then_inc(sa, 1)
            wait(e, sa, a0 + 1)
            e.activation(m[:, 2:3], m[:, 2:3], ACT.Exp, scale=-0.5).then_inc(sa, 1)
            wait(e, sd, d0 + 3)
            wait(e, sa, a0 + 2)
            e.activation(x, x, ACT.Identity, scale=m[:, 2:3], bias=m[:, 3:4]).then_inc(sa, 1)

        def store_x1(e, i):
            wait(e, s_n1d, NORM_D * (i + 1))
            e.dma_start(x1d[i * P:(i + 1) * P, :], X1[:, i, :]).then_inc(s_x1d, 16)

        def mixed_sp(e):
            wait(e, s_fd, 4 * 2)
            for kt in range(KT):
                e.dma_start(WO[kt], t["w_out"][kt]).then_inc(s_wo, 16)
            wait(e, s_fd, 4 * NPAIR)
            for k in range(2):
                e.dma_start(LN1[k], t["ln"][k:k + 1, :].broadcast_to([P, D])).then_inc(s_rc, 16)
            e.dma_start(rt_w, t["router_w"]).then_inc(s_rc, 16)
            e.dma_start(rt_b, t["router_b"].broadcast_to([P, E_N])).then_inc(s_rc, 16)
            for i in range(NT):
                if i >= 4:
                    store_x1(e, i - 4)
                if i == 3:
                    wait(e, s_mp, NB * MP)
                e.dma_start(XR[i % 4], t["x"][i * P:(i + 1) * P, :]).then_inc(s_xr[i % 4], 16)

        def out_pe(e, i):
            if i == 0:
                wait(e, s_nd, NPAIR)
                wait(e, s_wo, 16 * KT)
            if i >= 2:
                wait(e, s_n1d, NORM_D * (i - 2) + 1)
            for kts in ([x for x in range(KT) if x != NPAIR - 1], [NPAIR - 1]):
                if i == 0 and kts[0] == NPAIR - 1:
                    wait(e, s_fd, 4 * NPAIR)
                for half in range(2):
                    for kt in kts:
                        ins = e.matmul(PS[i % 2][:, half * HB:(half + 1) * HB], YT[:, kt, i * P:(i + 1) * P],
                                       WO[kt][:, half * HB:(half + 1) * HB], start=kt == 0, stop=kt == NPAIR - 1)
            ins.then_inc(s_op, 1)

        def out_dve(e, i):
            d0 = NORM_D * i
            x = XR[i % 4]
            if i == 0:
                wait(e, s_rc, 16 * 4)
            wait(e, s_op, i + 1)
            wait(e, s_xr[i % 4], 16 * (i // 4 + 1))
            e.scalar_tensor_tensor(x, x, ALPHA, PS[i % 2][:, :], ALU.mult, ALU.add).then_inc(s_n1d, 1)
            wait(e, s_n1d, d0 + 1)
            norm_dve(e, i, s_n1d, s_n1a, x, X1[:, i, :], LN1[0], LN1[1], d0 + 1, NORM_A * i)

        def logits_pe(e, i):
            wait(e, s_n1d, NORM_D * (i + 1))
            wait(e, s_x1t, i)
            for kt in range(KT):
                ins = e.transpose(PS[2][:, kt * P:(kt + 1) * P], X1[:, i, kt * P:(kt + 1) * P], ident[:, :])
            ins.then_inc(s_x1p, 1)
            wait(e, s_x1t, i + 1)
            for kt in range(KT):
                ins = e.matmul(PS[3][:, i * E_N:(i + 1) * E_N], X1T[:, kt * P:(kt + 1) * P],
                               rt_w[:, kt * E_N:(kt + 1) * E_N], start=kt == 0, stop=kt == KT - 1)
            ins.then_inc(s_lg, 1)

        def logits_act(e, i):
            wait(e, s_x1p, i + 1)
            wait(e, s_lg, i)
            e.copy(X1T, PS[2][:, :]).then_inc(s_x1t, 1)

        lg, pr, pm, am, pos = [small(NT * E_N) for _ in range(5)]
        oh12, k16_2 = small(2 * NT * E_N), small(2 * NT * E_N)
        oh1, oh2, k16 = oh12[:, 0:NT * E_N], oh12[:, NT * E_N:], k16_2[:, 0:NT * E_N]
        q1, q2, q3, g4, k4 = [small(NT * E_G) for _ in range(5)]
        c8 = [small(NT) for _ in range(3)]
        base = small((NT + 1) * E_N)
        first, last, nblk, b_end, b_sta, b_off, zero, b_row = [small(E_N) for _ in range(8)]
        n_int = small(E_N).bitcast(I32)
        place = small(2 * NT)
        place_i, place_b, place_r = [small(2 * NT).bitcast(I32) for _ in range(3)]
        row_hot = KB[:, 0:2, :].rearrange("p a b -> p (a b)")
        col_hot = KB[:, 2, 0:2 * NT * NCOL]
        assert roff[0] <= 3 * S

        def te(x):
            return x.rearrange("p (i e) -> p i e", e=E_N)

        def over(x, n):
            return x.rearrange("p (m o) -> p m o", o=1).broadcast_to([P, x.shape[1], n])

        def under(x, n):
            return x.rearrange("p (o m) -> p o m", o=1).broadcast_to([P, n, x.shape[1]])

        def router_pool(e):
            wait(e, s_fd, 4 * NPAIR)
            e.memset(ones, 1.0)
            e.memset(zero, 0.0)
            e.iota(rev4, [[-1, G_E]], base=G_E, channel_multiplier=0, allow_small_or_imprecise_dtypes=True)
            e.iota(rev16, [[-1, E_N]], base=E_N, channel_multiplier=0, allow_small_or_imprecise_dtypes=True)
            e.iota(blk_iota, [[1, MAXB + 1], [0, E_N]], base=0, channel_multiplier=0,
                   allow_small_or_imprecise_dtypes=True)
            e.iota(col_iota, [[1, NCOL]], base=0, channel_multiplier=0)
            e.iota(row_iota, [[1, P]], base=0, channel_multiplier=0)
            e.iota(token, [[P, NT]], base=0, channel_multiplier=1, allow_small_or_imprecise_dtypes=True)\
                .then_inc(s_rpool, 1)
            e.wait_ge(s_rpool, 1)
            e.affine_select(out=before, in_=ones, compare_op=ALU.is_gt, fill=0.0, base=0,
                            pattern=[[1, P]], channel_multiplier=-1).then_inc(s_rpool, 1)

        def router_dve(e):
            n = [0]

            def step(ins):
                ins.then_inc(s_q, 1)
                n[0] += 1
                e.wait_ge(s_q, n[0])
            TTo, RED = e.tensor_tensor, e.tensor_reduce
            wait(e, s_lg, NT)
            wait(e, s_rpool, 2)
            step(TTo(te(lg), te(PS[3][:, 0:NT * E_N]), under(rt_b, NT), ALU.add))
            step(RED(c8[0], te(lg), AX.X, ALU.max))
            TTo(te(lg), te(lg), over(c8[0], E_N), ALU.subtract).then_inc(s_qd, 1)
            e.wait_ge(s_qa, 1)
            step(RED(c8[0], te(pr), AX.X, ALU.add))
            step(e.reciprocal(c8[1], c8[0]))
            step(TTo(te(pr), te(pr), over(c8[1], E_N), ALU.mult))
            step(RED(q1, pr.rearrange("p (q e) -> p q e", e=G_E), AX.X, ALU.max))
            quad = lambda x: x.rearrange("p (q e) -> p q e", e=G_E)
            step(TTo(quad(k16), quad(pr), over(q1, G_E), ALU.is_equal))
            step(TTo(quad(k16), quad(k16), under(rev4, NT * E_G), ALU.mult))
            step(RED(q2, quad(k16), AX.X, ALU.max))
            step(TTo(quad(k16), quad(k16), over(q2, G_E), ALU.is_equal))
            step(e.scalar_tensor_tensor(pm, k16, -2.0, pr, ALU.mult, ALU.add))
            step(RED(q2, quad(pm), AX.X, ALU.max))
            step(TTo(q1, q1, q2, ALU.add))
            step(RED(c8[0], quad(q1), AX.X, ALU.max))
            step(TTo(quad(g4), quad(q1), over(c8[0], E_G), ALU.is_equal))
            step(TTo(quad(g4), quad(g4), under(rev4, NT), ALU.mult))
            step(RED(c8[1], quad(g4), AX.X, ALU.max))
            step(TTo(quad(g4), quad(g4), over(c8[1], E_G), ALU.is_equal))
            step(TTo(quad(pm), quad(pr), over(g4, G_E), ALU.mult))
            step(e.tensor_scalar_add(k4, g4, -1.0))
            step(TTo(quad(pm), quad(pm), over(k4, G_E), ALU.add))
            for k, oh in enumerate((oh1, oh2)):
                step(RED(c8[k], te(pm), AX.X, ALU.max))
                step(TTo(te(k16), te(pm), over(c8[k], E_N), ALU.is_equal))
                step(TTo(te(k16), te(k16), under(rev16, NT), ALU.mult))
                step(RED(c8[2], te(k16), AX.X, ALU.max))
                step(TTo(te(oh), te(k16), over(c8[2], E_N), ALU.is_equal))
                if k == 0:
                    step(e.scalar_tensor_tensor(pm, oh, -4.0, pm, ALU.mult, ALU.add))
            step(TTo(am, oh1, oh2, ALU.add))
            wait(e, s_q, n[0])
            e.memset(base[:, 0:E_N], 0.0).then_inc(s_qd, 1)
            step(TTo(c8[2], c8[0], c8[1], ALU.add))
            step(e.reciprocal(c8[2], c8[2]))
            for k in range(2):
                step(TTo(gate[:, k, :], c8[k], c8[2], ALU.mult))
            e.wait_ge(s_qp, 1)
            for i in range(NT):
                step(TTo(base[:, (i + 1) * E_N:(i + 2) * E_N], base[:, i * E_N:(i + 1) * E_N],
                         PS[2][:, i * E_N:(i + 1) * E_N], ALU.add))
            count = base[:, NT * E_N:]
            step(TTo(pos, PS[3][:, 0:NT * E_N], base[:, 0:NT * E_N], ALU.add))
            step(e.tensor_scalar_add(n_int, count, float(P - 1)))
            step(e.tensor_single_scalar(n_int, n_int, 7, ALU.logical_shift_right))
            step(e.tensor_scalar_max(nblk, n_int, 1.0))
            step(e.tensor_tensor_scan(b_end, nblk, zero, 0.0, ALU.add, ALU.add))
            step(TTo(b_sta, b_end, nblk, ALU.subtract))
            step(e.tensor_scalar_mul(b_row, b_sta, float(P)))
            step(TTo(te(lg), te(pos), under(b_row, NT), ALU.add))
            both = lambda x: x.rearrange("p (k m) -> p k m", k=2)
            twice = lambda x: x.rearrange("p (o m) -> p o m", o=1).broadcast_to([P, 2, NT * E_N])
            oh, k2 = oh12, k16_2
            step(TTo(both(k2), both(oh), twice(lg), ALU.mult))
            step(RED(place, te(k2), AX.X, ALU.add))
            step(e.tensor_copy(place_i, place))
            step(e.tensor_single_scalar(place_b, place_i, 7, ALU.logical_shift_right))
            step(e.tensor_single_scalar(place_r, place_i, P - 1, ALU.bitwise_and))
            ch = col_hot.rearrange("p (k c) -> p k c", c=NCOL)
            rh = row_hot.rearrange("p (k c) -> p k c", c=P)
            step(TTo(ch, under(col_iota, 2 * NT), over(place_b, NCOL), ALU.is_equal))
            tok2 = token.rearrange("p (o i n) -> p o i n", o=1, n=1).broadcast_to([P, 2, NT, NCOL])
            ch4 = col_hot.rearrange("p (k i c) -> p k i c", k=2, c=NCOL)
            step(TTo(ch4, ch4, tok2, ALU.mult))
            for k in range(2):
                TTo(rh[:, k * NT:(k + 1) * NT, :], under(row_iota, NT), over(place_r[:, k * NT:(k + 1) * NT], P),
                    ALU.is_equal).then_inc(s_hot, 1)
            step(e.tensor_copy(tab[:, 0:E_N], b_sta))
            e.tensor_copy(tab[:, E_N:E_N + 1], b_end[:, E_N - 1:E_N]).then_inc(s_tab, 1)
            step(e.tensor_tensor_scan(last, count, zero, 0.0, ALU.add, ALU.add))
            step(TTo(first, last, count, ALU.subtract))
            wait(e, s_idp, 1)
            e.tensor_copy(block_tok, PS[2][:, 256:256 + NCOL]).then_inc(s_idx, 1)
            step(TTo(te(lg), te(pos), under(first, NT), ALU.add))
            step(TTo(both(k2), both(oh), twice(lg), ALU.mult))
            step(RED(place, te(k2), AX.X, ALU.add))
            e.tensor_copy(slot.rearrange("p k i -> p (k i)"), place).then_inc(s_slot, 1)
            step(e.scalar_tensor_tensor(b_off, b_sta, float(-P), first, ALU.mult, ALU.add))
            W = MAXB + 1
            z1, z2 = KB[:, 5, 0:W * E_N], RW[:, 7, 0:W * E_N]
            r1 = RW[:, 4, 0:W]
            step(TTo(te(z1), te(blk_iota), under(b_sta, W), ALU.is_ge))
            step(TTo(te(z2), te(blk_iota), under(b_end, W), ALU.is_lt))
            step(TTo(z1, z1, z2, ALU.mult))
            step(TTo(te(z1), te(z1), under(b_off, W), ALU.mult))
            step(RED(r1, te(z1), AX.X, ALU.add))
            step(e.scalar_tensor_tensor(r1, te(blk_iota)[:, :, 0], float(P), r1, ALU.mult, ALU.add))
            step(e.tensor_scalar_min(r1, r1, float(ROWS - P)))
            e.tensor_copy(tab[:, 20:20 + W], r1).then_inc(s_row, 1)

        def router_act(e):
            e.wait_ge(s_qd, 1)
            e.activation(pr, lg, ACT.Exp).then_inc(s_qa, 1)
            e.wait_ge(s_x1d, 16 * NT)
            for i in range(NT):
                ins = e.mul(X1[:, i, :], X1[:, i, :], ALPHA)
            ins.then_inc(s_scaled, 1)

        def router_pe(e):
            e.wait_ge(s_qd, 2)
            e.matmul(PS[2][:, 0:NT * E_N], ones, am, start=True, stop=True)
            e.matmul(PS[3][:, 0:NT * E_N], before, am, start=True, stop=True).then_inc(s_qp, 1)
            for n in range(2 * NT):
                if n % NT == 0:
                    e.wait_ge(s_hot, n // NT + 1)
                ins = e.matmul(PS[2][:, 256:256 + NCOL], row_hot[:, n * P:(n + 1) * P],
                               col_hot[:, n * NCOL:(n + 1) * NCOL], start=n == 0, stop=n == 2 * NT - 1)
            ins.then_inc(s_idp, 1)

        x1d = nc.dram_tensor("x1d", (S, D), F32).ap()
        ys = nc.dram_tensor("ys", (ROWS, D), F32).ap()
        XSf = XS[:, :, :].rearrange("p a b -> p (a b)")
        RWf, KBf = RW[:, :, :].rearrange("p a b -> p (a b)"), KB[:, :, :].rearrange("p a b -> p (a b)")
        WSET = [[XSf[:, 0:4 * S], XSf[:, 4 * S:8 * S], XSf[:, 8 * S:12 * S]],
                [RWf[:, 0:4 * S], RWf[:, 4 * S:8 * S], KBf[:, 0:4 * S]]]
        Xg, XgT, Yb = YT[:, 0, :], YT[:, 1, :], YT[:, 4, :]
        Sg, Hh, HhT = YT[:, 2, 0:HB], YT[:, 2, HB:2 * HB], YT[:, 3, 0:HB]

        def load_expert(e, x, k):
            pick = (lambda w: w[x]) if isinstance(x, int) else (lambda w: w[bass.ds(x, 1)].rearrange("o a b -> (o a) b"))
            for j, name in enumerate(("w_gate", "w_upx", "w_down")):
                n = E_F if j < 2 else D
                e.dma_start(WSET[k][j].rearrange("p (a f) -> p a f", f=n),
                            pick(t[name]).rearrange("(a p) f -> p a f", p=P))\
                 .then_inc((s_wg, s_wu, s_wd)[j][k], 16)

        def table(e, at, hi, lo=0):
            return e.value_load(tab[0:1, bass.ds(at, 1)] if not isinstance(at, int) else tab[0:1, at:at + 1],
                                min_val=lo, max_val=hi)

        def expert_blocks(e, body, pairs=(0, E_N // 2), after=None):
            with e.Fori(*pairs) as ep:
                for k in range(2):
                    b0 = table(e, 2 * ep + k, MAXB)
                    b1 = table(e, 2 * ep + k + 1, MAXB, 1)
                    with e.Fori(b0, b1) as i:
                        body(i, k, ep)
                    if after is not None:
                        after(ep, k)

        def ahead(e, *sems):
            for x in sems:
                e.sem_inc(x)

        def moe_sp(e):
            ahead(e, s_ys)
            wait(e, s_mp, NB * MP)
            wait(e, s_bv, NU)
            wait(e, s_md, NB * MD)
            load_expert(e, 0, 0)
            for i in range(4, NT):
                store_x1(e, i)
            wait(e, s_op, NT)
            wait(e, s_row, 1)
            load_expert(e, 1, 1)
            for k in range(2):
                e.dma_start(LN2[k], t["ln"][2 + k:3 + k, :].broadcast_to([P, D])).then_inc(s_l2, 16)

            def store(i, k, ep):
                row = table(e, 20 + i, ROWS - P)
                e.wait_ge(s_ya, i + 2)
                e.wait_ge(s_yd, i + 2)
                e.sem_inc(s_tick[0])
                e.wait_ge(s_ys, i * 16 + 1)
                e.sem_inc(s_tick[0])
                e.dma_start(ys[bass.ds(row, P)], Yb).then_inc(s_ys, 16)
            expert_blocks(e, store, (0, E_N // 2 - 1), lambda ep, k: load_expert(e, 2 * ep + 2 + k, k))
            expert_blocks(e, store, (E_N // 2 - 1, E_N // 2))

        def moe_pool(e):
            e.wait_ge(s_idx, 1)
            e.wait_ge(s_x1d, 16 * NT)

            e.tensor_copy(cur_tok, block_tok[:, 0:1]).then_inc(s_pick, 1)
            e.wait_ge(s_pick, 1)
            e.indirect_dma_start(Xg, None, x1d, bass.IndirectOffsetOnAxis(cur_tok, 0)).then_inc(s_xg, 16)
            wait(e, s_tab, 1)
            total = table(e, E_N, MAXB, E_N)
            with e.Fori(1, total + 1) as i:
                e.wait_ge(s_xgp, i + 1)
                e.tensor_copy(cur_tok, block_tok[:, bass.ds(i, 1)]).then_inc(s_pick, 1)
                e.wait_ge(s_pick, i + 1)
                e.sem_inc(s_tick[1])
                e.indirect_dma_start(Xg, None, x1d, bass.IndirectOffsetOnAxis(cur_tok, 0)).then_inc(s_xg, 16)
            e.wait_ge(s_slot, 1)
            e.wait_ge(s_ys, total * 16 + 1)
            e.sem_inc(s_tick[1])
            for i in range(NT):
                for k in range(2):
                    n = 2 * i + k
                    e.indirect_dma_start(GATHERED[n], None, ys[0:2 * S, :],
                                         bass.IndirectOffsetOnAxis(slot[:, k, i:i + 1], 0)).then_inc(s_gt[n], 16)

        def xg_transposes(e):
            for kt in range(KT):
                ins = e.transpose(PS[1][:, kt * P:(kt + 1) * P], Xg[:, kt * P:(kt + 1) * P], ident[:, :])
            ins.then_inc(s_xgp, 1)

        def moe_pe(e):
            ahead(e, s_xgp, s_htp, s_htp2, s_y1)
            e.wait_ge(s_xg, 16)
            xg_transposes(e)
            e.wait_ge(s_tab, 1)

            def body(i, k, ep):
                wg, wu, wd = WSET[k]
                e.wait_ge(s_wg[k], 16 * (ep + 1))
                e.wait_ge(s_ta, i + 1)
                e.wait_ge(s_td, i + 1)
                e.wait_ge(s_hd2, i + 1)
                for kt in range(KT):
                    ins = e.matmul(PS[0][:, 0:HB], XgT[:, kt * P:(kt + 1) * P], wg[:, kt * E_F:(kt + 1) * E_F],
                                   start=kt == 0, stop=kt == KT - 1)
                ins.then_inc(s_g1, 1)
                e.wait_ge(s_wu[k], 16 * (ep + 1))
                for kt in range(KT):
                    ins = e.matmul(PS[0][:, HB:2 * HB], XgT[:, kt * P:(kt + 1) * P], wu[:, kt * E_F:(kt + 1) * E_F],
                                   start=kt == 0, stop=kt == KT - 1)
                ins.then_inc(s_u1, 1)
                e.wait_ge(s_xg, 16 * (i + 2))
                xg_transposes(e)
                e.wait_ge(s_hd, i + 2)
                e.wait_ge(s_htd, i + 1)
                for f in range(2):
                    ins = e.transpose(PS[2][:, f * P:(f + 1) * P], Hh[:, f * P:(f + 1) * P], ident[:, :])
                ins.then_inc(s_htp, 1)
                e.wait_ge(s_hd2, i + 2)
                e.wait_ge(s_hta, i + 1)
                for f in range(2, FT):
                    ins = e.transpose(PS[2][:, f * P + HB - 2 * P:(f + 1) * P + HB - 2 * P], Hh[:, f * P:(f + 1) * P],
                                      ident[:, :])
                ins.then_inc(s_htp2, 1)
                e.wait_ge(s_wd[k], 16 * (ep + 1))
                e.wait_ge(s_ya, i + 1)
                e.wait_ge(s_yd, i + 1)
                e.wait_ge(s_htd, i + 2)
                for half in range(2):
                    for f in range(FT):
                        if half == 0 and f == 2:
                            e.wait_ge(s_hta, i + 2)
                        ins = e.matmul(PS[3][:, half * HB:(half + 1) * HB], HhT[:, f * P:(f + 1) * P],
                                       wd[:, f * D + half * HB:f * D + (half + 1) * HB], start=f == 0, stop=f == FT - 1)
                ins.then_inc(s_y1, 1)
            expert_blocks(e, body)

        def moe_act(e):
            ahead(e, s_ya, s_hta)
            e.wait_ge(s_xgp, 2)
            e.copy(XgT[:, 0:HB], PS[1][:, 0:HB]).then_inc(s_ta, 1)

            def body(i, k, ep):
                e.wait_ge(s_g1, i + 1)
                e.wait_ge(s_hd2, i + 1)
                e.activation(Sg, PS[0][:, 0:HB], ACT.Silu).then_inc(s_si, 1)
                e.wait_ge(s_htp2, i + 2)
                e.wait_ge(s_y1, i + 1)
                e.copy(HhT[:, 2 * P:4 * P], PS[2][:, HB:HB + 2 * P]).then_inc(s_hta, 1)
                e.wait_ge(s_xgp, i + 3)
                e.copy(XgT[:, 0:HB], PS[1][:, 0:HB]).then_inc(s_ta, 1)
                e.wait_ge(s_y1, i + 2)
                e.wait_ge(s_ys, i * 16 + 1)
                e.copy(Yb[:, 0:HB], PS[3][:, 0:HB]).then_inc(s_ya, 1)
            expert_blocks(e, body)

        def moe_dve(e):
            ahead(e, s_hd, s_hd2, s_yd, s_htd)
            e.wait_ge(s_xgp, 2)
            e.tensor_copy(XgT[:, HB:2 * HB], PS[1][:, HB:2 * HB]).then_inc(s_td, 1)

            def body(i, k, ep):
                e.wait_ge(s_u1, i + 1)
                e.wait_ge(s_si, i + 1)
                e.wait_ge(s_htp2, i + 1)
                for f, done in ((0, s_hd), (2, s_hd2)):
                    e.tensor_tensor(Hh[:, f * P:(f + 2) * P], Sg[:, f * P:(f + 2) * P],
                                    PS[0][:, HB + f * P:HB + (f + 2) * P], ALU.mult).then_inc(done, 1)
                e.wait_ge(s_htp, i + 2)
                e.wait_ge(s_y1, i + 1)
                e.tensor_copy(HhT[:, 0:2 * P], PS[2][:, 0:2 * P]).then_inc(s_htd, 1)
                e.wait_ge(s_xgp, i + 3)
                e.tensor_copy(XgT[:, HB:2 * HB], PS[1][:, HB:2 * HB]).then_inc(s_td, 1)
                e.wait_ge(s_y1, i + 2)
                e.wait_ge(s_ys, i * 16 + 1)
                e.tensor_copy(Yb[:, HB:2 * HB], PS[3][:, HB:2 * HB]).then_inc(s_yd, 1)
            expert_blocks(e, body)

        N2_A = 3
        GATHERED = [XS[:, n, :] for n in range(12)] + [RW[:, n, :] for n in range(4)]

        def final_sum(e, i):
            x, st = X1[:, i, :], stats[:, i % 2, :]
            for k in range(2):
                wait(e, s_gt[2 * i + k], 16)
                wait(e, s_f1, 4 * i + k)
                e.scalar_tensor_tensor(x, GATHERED[2 * i + k], gate[:, k, i:i + 1], x, ALU.mult, ALU.add)\
                    .then_inc(s_f1, 1)
                if k == 0 and i > 0:
                    final_bias(e, i - 1)
            wait(e, s_f1, 4 * i + 2)
            for half in range(2):
                ins = e.bn_stats(st[:, 6 * half:6 * half + 6], x[:, half * HB:(half + 1) * HB])
            ins.then_inc(s_f1, 1)
            wait(e, s_f1, 4 * i + 3)
            e.bn_aggr(mv[:, i % 2, 0:2], st).then_inc(s_f1, 1)

        def final_bias(e, i):
            m = mv[:, i % 2, :]
            wait(e, s_f1, 4 * i + 4)
            wait(e, s_n2a, N2_A * i + 2)
            e.scalar_tensor_tensor(m[:, 3:4], m[:, 0:1], -1.0, m[:, 2:3], ALU.mult, ALU.mult).then_inc(s_f2, 1)

        def final_dve(e):
            e.wait_ge(s_l2, 32)
            e.wait_ge(s_scaled, 1)
            for i in range(NT + 1):
                if i < NT:
                    final_sum(e, i)
                else:
                    final_bias(e, i - 1)
                if i > 0:
                    x = X1[:, i - 1, :]
                    wait(e, s_n2a, N2_A * i)
                    e.tensor_tensor(x, x, LN2[0], ALU.mult).then_inc(s_f3, 1)

        def final_act(e, i):
            x, m, a0 = X1[:, i, :], mv[:, i % 2, :], N2_A * i
            wait(e, s_n2a, a0)
            wait(e, s_f1, 4 * i + 4)
            e.activation(m[:, 2:3], m[:, 1:2], ACT.Ln, bias=consts[:, 3:4]).then_inc(s_n2a, 1)
            wait(e, s_n2a, a0 + 1)
            e.activation(m[:, 2:3], m[:, 2:3], ACT.Exp, scale=-0.5).then_inc(s_n2a, 1)
            wait(e, s_n2a, a0 + 2)
            wait(e, s_f2, i + 1)
            e.activation(x, x, ACT.Identity, scale=m[:, 2:3], bias=m[:, 3:4]).then_inc(s_n2a, 1)

        def final_pool(e, i):
            x = X1[:, i, :]
            wait(e, s_f3, i + 1)
            e.tensor_tensor(x, x, LN2[1], ALU.add).then_inc(s_f4, 1)

        def final_sp(e):
            for i in range(NT):
                wait(e, s_f4, i + 1)
                e.dma_start(out[0, i * P:(i + 1) * P, :], X1[:, i, :]).then_inc(s_out, 16)
            e.wait_ge(s_out, 16 * NT)

        @block.sync
        def _(e):
            proj_sp(e)
            mixed_sp(e)
            moe_sp(e)
            final_sp(e)

        @block.gpsimd
        def _(e):
            masks_pool(e)
            mats_pool(e)
            router_pool(e)
            moe_pool(e)
            for i in range(NT):
                final_pool(e, i)

        LRU_AT = [LRU_T + 3 * u for u in range(2)]
        RW_AT = [RW_END + 3 * g for g in range(NPAIR)]
        PE_AFTER, ACT_AFTER, LRU_DVE_AFTER = {}, {RW_END - 1: [(rw_pre_act,)]}, {}
        for u, n in enumerate(LRU_AT):
            PE_AFTER[n] = [(lru_pe, u, 0), (lru_pe, u, 1)]
            PE_AFTER[n + 2] = [(lru_pe, u, 2)]
            for part in range(3):
                ACT_AFTER[n + part] = [(lru_act, u, part)]
                LRU_DVE_AFTER[n + part] = u
        for g, n in enumerate(RW_AT):
            for part in range(3):
                PE_AFTER[n + part] = [(rw_pe, g, part)]
            for part in range(2):
                ACT_AFTER[n + part] = [(rw_act, g, part)]

        @block.scalar
        def _(e):
            lam_act(e)
            for n in range(CT + NT):
                proj_act(e, n)
                for f, *args in ACT_AFTER.get(n, ()):
                    f(e, *args)
            for b in range(NB):
                side_by_side(mats_act, sba_act, e, b)
                if b % NQ == NQ - 1:
                    rnorm_act(e, b // NQ)
            for i in range(NT):
                norm_act(e, i, s_n1d, s_n1a, XR[i % 4], NORM_D * i + 1, NORM_A * i)
                if i >= 1:
                    logits_act(e, i - 1)
            logits_act(e, NT - 1)
            router_act(e)
            moe_act(e)
            exp_ln(e)
            for i in range(NT):
                final_act(e, i)

        @block.vector
        def _(e):
            masks_dve(e)
            lru = [lru_dve(e, u) for u in range(2)]
            next(lru[0])
            for r in range(RW_T):
                proj_dve(e, r)
                u = LRU_DVE_AFTER.get(r + LRU_T)
                if u is not None:
                    next(lru[u], None)
                    if u == 0 and r + LRU_T == LRU_AT[0] + 2:
                        next(lru[1])
            for g in range(NPAIR):
                rw_dve(e, g)
            for b in range(NB):
                u = (batch_step(b) + GAPS - 1) // 4
                side_by_side(mats_dve, lambda e, j: sba_dve(e, j, j < 4 * u), e, b)
                if u < NU:
                    sba_scan(e, u)
                if b % NQ == NQ - 1:
                    rnorm_dve(e, b // NQ)
            for i in range(NT):
                out_dve(e, i)
            router_dve(e)
            moe_dve(e)
            final_dve(e)

        @block.tensor
        def _(e):
            for n in range(CT + NT):
                proj_pe(e, n)
                for f, *args in PE_AFTER.get(n, ()):
                    f(e, *args)
            for b in range(NB):
                side_by_side(mats_pe, sba_pe, e, b)
                if b % NQ == NQ - 1:
                    rnorm_pe(e, b // NQ)
            for i in range(NT):
                out_pe(e, i)
                if i >= 2:
                    logits_pe(e, i - 2)
            logits_pe(e, NT - 2)
            logits_pe(e, NT - 1)
            router_pe(e)
            moe_pe(e)


def lay_out(inputs, np):
    f = {k: np.asarray(v) for k, v in inputs.items()}
    tiles = lambda a: a.reshape(-1, P).T
    vecs = [tiles(f[k]) for k in ("shift_mu", "rwkv_w0", "rwkv_a0", "rwkv_k_k", "rwkv_k_a", "rwkv_r_k", "rwkv_ln_g",
                                  "rwkv_ln_b", "sba_norm_g", "lru_conv_w", "lru_conv_b", "lru_ba", "lru_bx",
                                  "lru_lambda", "lru_norm_g")]
    w = f["w_in"][0].reshape(KT, P, IN_COLS)
    lru = np.stack([f[k][0].reshape(2, 2, HD, HD) for k in ("lru_wa", "lru_wx")])
    order = [*range(RW_T, RW_END), *range(RW_T), *range(RW_END, CT)]
    a = {
        "x": f["x"][0],
        "xT": f["x"][0].T.reshape(KT, P, S),
        "w_in": w[:, :, :V_COL].reshape(KT, P, CT, P).transpose(2, 1, 0, 3).reshape(CT, P, D)[order],
        "w_v": w[:, :, V_COL:].transpose(1, 0, 2).reshape(P, KT * SBA_W),
        "vecs": np.concatenate(vecs, axis=1),
        "lora_up": np.concatenate([f["rwkv_w_up"][0], f["rwkv_a_up"][0]], axis=0),
        "g_up": f["rwkv_g_up"][0],
        "lru_w": lru.transpose(2, 3, 0, 1, 4).reshape(P, 2, 2, HD),
        "w_out": f["w_out"][0].reshape(KT, P, D),
        "ln": np.stack([f[k][0] for k in ("ln1_g", "ln1_b", "ln2_g", "ln2_b")]),
        "router_w": f["router_w"].reshape(KT, P, E_N).transpose(1, 0, 2).reshape(P, KT * E_N),
        "router_b": f["router_b"].reshape(1, E_N),
        "w_gate": f["exp_w_gate"][0],
        "w_upx": f["exp_w_up"][0],
        "w_down": f["exp_w_down"][0],
    }
    return {k: np.ascontiguousarray(v) for k, v in a.items()}


def kernel(**inputs):
    import numpy as np
    import concourse.bacc as bacc
    from concourse.bass_utils import run_bass_kernel_spmd

    nc = bacc.Bacc("TRN2", target_bir_lowering=False, num_devices=1)
    arrays = {f"in_{k}": v for k, v in lay_out(inputs, np).items()}
    t = {k[3:]: nc.dram_tensor(k, v.shape, mybir.dt.from_np(v.dtype), kind="ExternalInput").ap()
         for k, v in arrays.items()}
    out = nc.dram_tensor("out", (1, S, D), F32, kind="ExternalOutput").ap()
    layer_kernel(nc, t, out)
    r = run_bass_kernel_spmd(nc, [arrays], core_ids=[0])
    return r.results[0]["out"]
```
